# Optimizing a Trainium2 kernel written in Bass

```python
import jax, jax.numpy as jnp
from jax import lax
import numpy as np

D_MODEL = 1024
BATCH = 1
SEQ = 256
DEPTH = 2

HEAD_DIM = 64
ATTN_Q_HEADS = 8
ATTN_KV_HEADS = 2
ATTN_GROUP = ATTN_Q_HEADS // ATTN_KV_HEADS
WINDOW = 128
ATTN_BLOCK = 128
ROPE_THETA = 10000.0
ATTN_WIDTH = ATTN_Q_HEADS * HEAD_DIM
KV_WIDTH = ATTN_KV_HEADS * HEAD_DIM
CONV_WIDTH = D_MODEL // 2
SHORT_CONV_K = 3
HY_SPLITS = (ATTN_WIDTH, KV_WIDTH, KV_WIDTH, CONV_WIDTH, CONV_WIDTH, CONV_WIDTH)
HY_IN_WIDTH = sum(HY_SPLITS)
HY_OUT_WIDTH = ATTN_WIDTH + CONV_WIDTH
GLA_HEADS = 4
GLA_KEY_DIM = D_MODEL // 2
GLA_VAL_DIM = D_MODEL
GLA_DK = GLA_KEY_DIM // GLA_HEADS
GLA_DV = GLA_VAL_DIM // GLA_HEADS
GLA_GATE_RANK = 16
GLA_GATE_NORMALIZER = 16.0
GLA_CHUNK = 64
GLA_SPLITS = (GLA_KEY_DIM, GLA_KEY_DIM, GLA_VAL_DIM, GLA_GATE_RANK, GLA_VAL_DIM)
GLA_IN_WIDTH = sum(GLA_SPLITS)
D_FF = 2816
FFN_CONV_K = 3
PLE_DIM = 256
MAX_POS_OFFSET = 1024
N_EVEN = (DEPTH + 1) // 2
N_ODD = DEPTH // 2
RMS_EPS = 1e-6


def _split(z, widths):
    idx, acc = [], 0
    for w in widths[:-1]:
        acc += w
        idx.append(acc)
    return jnp.split(z, idx, axis=-1)

def _rms_norm(x, gain):
    xf = x.astype(jnp.float32)
    y = xf * lax.rsqrt(jnp.mean(xf * xf, axis=-1, keepdims=True) + RMS_EPS)
    return (y * gain.astype(jnp.float32)).astype(x.dtype)

def _causal_depthwise_conv(x, w):
    k = w.shape[0]
    return lax.conv_general_dilated(
        x, w[:, None, :].astype(x.dtype), window_strides=(1,), padding=[(k - 1, 0)],
        dimension_numbers=('NWC', 'WIO', 'NWC'), feature_group_count=x.shape[-1])

def _rope_tables(positions):
    inv_freq = ROPE_THETA ** (-jnp.arange(0, HEAD_DIM, 2, dtype=jnp.float32) / HEAD_DIM)
    ang = positions.astype(jnp.float32)[..., None] * inv_freq
    return jnp.cos(ang)[:, :, None, :], jnp.sin(ang)[:, :, None, :]

def _apply_rope(x, cos, sin):
    x1, x2 = jnp.split(x.astype(jnp.float32), 2, axis=-1)
    return jnp.concatenate([x1 * cos - x2 * sin, x2 * cos + x1 * sin], axis=-1).astype(x.dtype)

def _sliding_window_sink_attention(q, k, v, sinks):
    b, s = q.shape[0], q.shape[1]
    nb = s // ATTN_BLOCK
    qb = q.reshape(b, nb, ATTN_BLOCK, ATTN_KV_HEADS, ATTN_GROUP, HEAD_DIM)

    def band(t):
        tb = t.reshape(b, nb, ATTN_BLOCK, ATTN_KV_HEADS, HEAD_DIM)
        prev = jnp.pad(tb[:, :-1], ((0, 0), (1, 0), (0, 0), (0, 0), (0, 0)))
        return jnp.concatenate([prev, tb], axis=2)

    kband, vband = band(k), band(v)
    scores = jnp.einsum('bnqhgd,bnkhd->bnhgqk', qb, kband).astype(jnp.float32) * (HEAD_DIM ** -0.5)
    blk = jnp.arange(nb)[:, None] * ATTN_BLOCK
    q_pos = blk + jnp.arange(ATTN_BLOCK)[None, :]
    k_pos = blk - ATTN_BLOCK + jnp.arange(2 * ATTN_BLOCK)[None, :]
    dist = q_pos[:, :, None] - k_pos[:, None, :]
    allowed = (dist >= 0) & (dist < WINDOW) & (k_pos[:, None, :] >= 0)
    scores = jnp.where(allowed[None, :, None, None], scores, -jnp.inf)
    sink = jnp.broadcast_to(
        sinks.astype(jnp.float32).reshape(1, 1, ATTN_KV_HEADS, ATTN_GROUP, 1, 1), scores.shape[:-1] + (1,))
    probs = jax.nn.softmax(jnp.concatenate([scores, sink], axis=-1), axis=-1)[..., :-1]
    out = jnp.einsum('bnhgqk,bnkhd->bnqhgd', probs.astype(v.dtype), vband)
    return out.reshape(b, s, ATTN_WIDTH)

def _attn_conv_mixer(h, cos, sin, w_in, q_norm, k_norm, sinks, conv_w, w_out):
    b, s, _ = h.shape
    q, k, v, cb, cc, cx = _split(h @ w_in, HY_SPLITS)
    q = _apply_rope(_rms_norm(q.reshape(b, s, ATTN_Q_HEADS, HEAD_DIM), q_norm), cos, sin)
    k = _apply_rope(_rms_norm(k.reshape(b, s, ATTN_KV_HEADS, HEAD_DIM), k_norm), cos, sin)
    v = v.reshape(b, s, ATTN_KV_HEADS, HEAD_DIM)
    attn = _sliding_window_sink_attention(q, k, v, sinks)
    conv = cb * _causal_depthwise_conv(cc * cx, conv_w)
    return jnp.concatenate([attn, conv], axis=-1) @ w_out

def _gla_chunked(q, k, v, log_a):
    b, s, nh, dk = q.shape
    dv = v.shape[-1]
    nc = s // GLA_CHUNK

    def chunks(t):
        return t.astype(jnp.float32).reshape(b, nc, GLA_CHUNK, nh, t.shape[-1]).transpose(1, 0, 3, 2, 4)

    qc, kc, vc = chunks(q), chunks(k), chunks(v)
    gc = jnp.cumsum(chunks(log_a), axis=3)
    causal = jnp.tril(jnp.ones((GLA_CHUNK, GLA_CHUNK), dtype=bool))

    def step(state, inp):
        qi, ki, vi, gi = inp
        g_end = gi[:, :, -1, :]
        o_inter = jnp.einsum('bhtd,bhdv->bhtv', qi * jnp.exp(gi), state)
        rel = gi[:, :, :, None, :] - gi[:, :, None, :, :]
        decay = jnp.exp(jnp.where(causal[:, :, None], rel, -jnp.inf))
        scores = jnp.einsum('bhtd,bhsd,bhtsd->bhts', qi, ki, decay)
        o_intra = jnp.einsum('bhts,bhsv->bhtv', scores, vi)
        state = jnp.exp(g_end)[..., None] * state + jnp.einsum(
            'bhsd,bhsv->bhdv', ki * jnp.exp(g_end[:, :, None, :] - gi), vi)
        return state, o_inter + o_intra

    state0 = jnp.zeros((b, nh, dk, dv), jnp.float32)
    _, o = lax.scan(step, state0, (qc, kc, vc, gc))
    return o.transpose(1, 0, 3, 2, 4).reshape(b, s, nh, dv)

def _gla_mixer(h, w_in, w_gate_up, gate_bias, o_norm, w_out):
    b, s, _ = h.shape
    q, k, v, g_lr, og = _split(h @ w_in, GLA_SPLITS)
    log_a = jax.nn.log_sigmoid((g_lr @ w_gate_up + gate_bias).astype(jnp.float32)) / GLA_GATE_NORMALIZER

    def heads(t, d):
        return t.reshape(b, s, GLA_HEADS, d)

    o = _gla_chunked(heads(q, GLA_DK) * (GLA_DK ** -0.5), heads(k, GLA_DK), heads(v, GLA_DV), heads(log_a, GLA_DK))
    o = _rms_norm(o.astype(h.dtype), o_norm) * jax.nn.silu(heads(og, GLA_DV))
    return o.reshape(b, s, GLA_VAL_DIM) @ w_out

def _conv_ffn(h, w_up, conv_w, conv_b, w_down):
    u = _causal_depthwise_conv(h @ w_up, conv_w) + conv_b
    gate, up = jnp.split(u, 2, axis=-1)
    return (jax.nn.gelu(gate, approximate=False) * up) @ w_down

def _per_layer_embedding(x, p_i, norm, w_gate, w_proj):
    gate = jax.nn.sigmoid(_rms_norm(x, norm) @ w_gate)
    return gate * (p_i @ w_proj)

def first_inputs(seed: int = 0) -> dict:
    key = jax.random.key(seed)
    ks = jax.random.split(key, 24)
    f32 = jnp.float32

    def normal(k, shape, fan_in):
        return jax.random.normal(k, shape, f32) * (fan_in ** -0.5)

    def gain(k, shape):
        return 1.0 + 0.05 * jax.random.normal(k, shape, f32)

    x = jax.random.normal(ks[0], (BATCH, SEQ, D_MODEL), f32)
    p = jax.random.normal(ks[1], (DEPTH, BATCH, SEQ, PLE_DIM), f32)
    offset = jax.random.randint(ks[2], (BATCH, 1), 0, MAX_POS_OFFSET, dtype=jnp.int32)
    positions = offset + jnp.arange(SEQ, dtype=jnp.int32)[None, :]
    return {
        'x': x,
        'p': p,
        'positions': positions,
        'mix_norm': gain(ks[3], (DEPTH, D_MODEL)),
        'ffn_norm': gain(ks[4], (DEPTH, D_MODEL)),
        'ffn_w_up': normal(ks[5], (DEPTH, D_MODEL, 2 * D_FF), D_MODEL),
        'ffn_conv_w': normal(ks[6], (DEPTH, FFN_CONV_K, 2 * D_FF), FFN_CONV_K),
        'ffn_conv_b': 0.02 * jax.random.normal(ks[7], (DEPTH, 2 * D_FF), f32),
        'ffn_w_down': normal(ks[8], (DEPTH, D_FF, D_MODEL), D_FF),
        'ple_norm': gain(ks[9], (DEPTH, D_MODEL)),
        'ple_w_gate': normal(ks[10], (DEPTH, D_MODEL, D_MODEL), D_MODEL),
        'ple_w_proj': normal(ks[11], (DEPTH, PLE_DIM, D_MODEL), PLE_DIM),
        'hy_w_in': normal(ks[12], (N_EVEN, D_MODEL, HY_IN_WIDTH), D_MODEL),
        'hy_q_norm': gain(ks[13], (N_EVEN, HEAD_DIM)),
        'hy_k_norm': gain(ks[14], (N_EVEN, HEAD_DIM)),
        'hy_sinks': jax.random.normal(ks[15], (N_EVEN, ATTN_Q_HEADS), f32),
        'hy_conv_w': normal(ks[16], (N_EVEN, SHORT_CONV_K, CONV_WIDTH), SHORT_CONV_K),
        'hy_w_out': normal(ks[17], (N_EVEN, HY_OUT_WIDTH, D_MODEL), HY_OUT_WIDTH),
        'gla_w_in': normal(ks[18], (N_ODD, D_MODEL, GLA_IN_WIDTH), D_MODEL),
        'gla_w_gate_up': normal(ks[19], (N_ODD, GLA_GATE_RANK, GLA_KEY_DIM), GLA_GATE_RANK),
        'gla_gate_bias': 0.1 * jax.random.normal(ks[20], (N_ODD, GLA_KEY_DIM), f32),
        'gla_o_norm': gain(ks[21], (N_ODD, GLA_DV)),
        'gla_w_out': normal(ks[22], (N_ODD, GLA_VAL_DIM, D_MODEL), GLA_VAL_DIM),
    }

def first_block(x, p, positions, mix_norm, ffn_norm, ffn_w_up, ffn_conv_w, ffn_conv_b, ffn_w_down,
              ple_norm, ple_w_gate, ple_w_proj, hy_w_in, hy_q_norm, hy_k_norm, hy_sinks, hy_conv_w,
              hy_w_out, gla_w_in, gla_w_gate_up, gla_gate_bias, gla_o_norm, gla_w_out):
    cos, sin = _rope_tables(positions)
    for i in range(DEPTH):
        j = i // 2
        h = _rms_norm(x, mix_norm[i])
        if i % 2 == 0:
            x = x + _attn_conv_mixer(h, cos, sin, hy_w_in[j], hy_q_norm[j], hy_k_norm[j], hy_sinks[j],
                                     hy_conv_w[j], hy_w_out[j])
        else:
            x = x + _gla_mixer(h, gla_w_in[j], gla_w_gate_up[j], gla_gate_bias[j], gla_o_norm[j], gla_w_out[j])
        x = x + _conv_ffn(_rms_norm(x, ffn_norm[i]), ffn_w_up[i], ffn_conv_w[i], ffn_conv_b[i], ffn_w_down[i])
        x = x + _per_layer_embedding(x, p[i], ple_norm[i], ple_w_gate[i], ple_w_proj[i])
    return x


DEPTH_2 = 1

GRID_W = 64
CTX_LEN = 256
N_HEADS = 8
N_KV_HEADS = 2
HEAD_DIM_2 = 128
Q_BLOCK = 128
CONV_DIM = 512
CONV_WIDTH_2 = 31
FFN_DIM = 2816
FFN_CONV_WIDTH = 3
EPS = 1e-6
Q_DIM = N_HEADS * HEAD_DIM_2
KV_DIM = N_KV_HEADS * HEAD_DIM_2
IN_DIM = Q_DIM + 2 * KV_DIM + 2 * CONV_DIM + 2 * D_MODEL
SPLITS = (Q_DIM, Q_DIM + KV_DIM, Q_DIM + 2 * KV_DIM, Q_DIM + 2 * KV_DIM + 2 * CONV_DIM)


def rms_norm(x, g):
    xf = x.astype(jnp.float32)
    y = xf * lax.rsqrt(jnp.mean(xf * xf, axis=-1, keepdims=True) + EPS)
    return (y * g.astype(jnp.float32)).astype(x.dtype)

def layer_norm(x, g, b):
    xf = x.astype(jnp.float32)
    mu = jnp.mean(xf, axis=-1, keepdims=True)
    var = jnp.mean(jnp.square(xf - mu), axis=-1, keepdims=True)
    y = (xf - mu) * lax.rsqrt(var + EPS)
    return (y * g.astype(jnp.float32) + b.astype(jnp.float32)).astype(x.dtype)

def depthwise_conv(x, w, b):
    C = x.shape[-1]
    y = lax.conv_general_dilated(x, w[:, None, :], window_strides=(1,), padding='SAME',
                                 dimension_numbers=('NWC', 'WIO', 'NWC'), feature_group_count=C)
    return y + b

def modulation(cvec, w_mod, b_mod):
    m = jax.nn.silu(cvec) @ w_mod + b_mod
    return jnp.split(m[:, None, :], 6, axis=-1)

def modulate(h, shift, scale):
    return h * (1.0 + scale) + shift

def axial_rope(rows):
    half = HEAD_DIM_2 // 2
    inv_freq = ROPE_THETA ** (-jnp.arange(0, half, 2, dtype=jnp.float32) / half)
    r = jnp.repeat(jnp.arange(rows, dtype=jnp.float32), GRID_W)
    col = jnp.tile(jnp.arange(GRID_W, dtype=jnp.float32), rows)
    ang = jnp.concatenate([r[:, None] * inv_freq, col[:, None] * inv_freq], axis=-1)
    return jnp.cos(ang), jnp.sin(ang)

def apply_rope(x, cos, sin):
    xf = x.astype(jnp.float32).reshape(x.shape[:-1] + (HEAD_DIM_2 // 2, 2))
    x0, x1 = xf[..., 0], xf[..., 1]
    c = cos[None, :, None, :]
    s = sin[None, :, None, :]
    out = jnp.stack([x0 * c - x1 * s, x0 * s + x1 * c], axis=-1)
    return out.reshape(x.shape).astype(x.dtype)

def head_rms(t, n_heads, g):
    B, L, _ = t.shape
    return rms_norm(t.reshape(B, L, n_heads, HEAD_DIM_2), g)

def project(h, w_in, q_g, k_g):
    p = h @ w_in
    q, k, v, u, g = jnp.split(p, SPLITS, axis=-1)
    B, L, _ = h.shape
    q = head_rms(q, N_HEADS, q_g)
    k = head_rms(k, N_KV_HEADS, k_g)
    v = v.reshape(B, L, N_KV_HEADS, HEAD_DIM_2)
    return q, k, v, u, g

def context_kv(hc, w_in, k_g):
    p = hc @ w_in[:, Q_DIM:Q_DIM + 2 * KV_DIM]
    k, v = jnp.split(p, 2, axis=-1)
    B, L, _ = hc.shape
    return head_rms(k, N_KV_HEADS, k_g), v.reshape(B, L, N_KV_HEADS, HEAD_DIM_2)

def block_attention(q, k, v):
    B, Lq, H, d = q.shape
    G = H // N_KV_HEADS
    nblk = Lq // Q_BLOCK
    qb = q.reshape(B, nblk, Q_BLOCK, N_KV_HEADS, G, d).transpose(1, 0, 2, 3, 4, 5)
    scale = HEAD_DIM_2 ** -0.5

    def one_block(qblk):
        s = jnp.einsum('bqkgd,bskd->bkgqs', qblk, k, preferred_element_type=jnp.float32) * scale
        p = jax.nn.softmax(s, axis=-1)
        return jnp.einsum('bkgqs,bskd->bqkgd', p.astype(v.dtype), v)

    o = lax.map(one_block, qb)
    return o.transpose(1, 0, 2, 3, 4, 5).reshape(B, Lq, H * d)

def conformer_conv(u, dw_w, dw_b, ln_g, ln_b, w_conv_out):
    a, b = jnp.split(u, 2, axis=-1)
    h = a * jax.nn.sigmoid(b)
    h = depthwise_conv(h, dw_w, dw_b)
    h = jax.nn.silu(layer_norm(h, ln_g, ln_b))
    return h @ w_conv_out

def merge_branches(attn, u, g, w_attn_out, dw_w, dw_b, ln_g, ln_b, w_conv_out, w_out):
    y_a = attn @ w_attn_out
    y_b = conformer_conv(u, dw_w, dw_b, ln_g, ln_b, w_conv_out)
    g_a, g_b = jnp.split(g, 2, axis=-1)
    return (jax.nn.sigmoid(g_a) * y_a + jax.nn.sigmoid(g_b) * y_b) @ w_out

def conv_glu_ffn(h, w_up, dw_w, dw_b, w_down):
    up = h @ w_up
    a, b = jnp.split(up, 2, axis=-1)
    a = depthwise_conv(a, dw_w, dw_b)
    return (jax.nn.gelu(a, approximate=True) * b) @ w_down

def second_inputs(seed: int = 0) -> dict:
    key = jax.random.key(seed)
    ks = jax.random.split(key, 24)

    def nrm(k, shape, scale):
        return jax.random.normal(k, shape, jnp.float32) * scale

    return {
        'x': nrm(ks[0], (BATCH, SEQ, D_MODEL), 1.0),
        'c': nrm(ks[1], (BATCH, D_MODEL), 1.0),
        'ctx': nrm(ks[2], (BATCH, CTX_LEN, D_MODEL), 1.0),
        'c_ctx': nrm(ks[3], (D_MODEL,), 1.0),
        'w_mod': nrm(ks[4], (DEPTH_2, D_MODEL, 6 * D_MODEL), 0.5 * D_MODEL ** -0.5),
        'b_mod': nrm(ks[5], (DEPTH_2, 6 * D_MODEL), 0.02),
        'norm1_g': 1.0 + nrm(ks[6], (DEPTH_2, D_MODEL), 0.02),
        'w_in': nrm(ks[7], (DEPTH_2, D_MODEL, IN_DIM), D_MODEL ** -0.5),
        'q_norm_g': 1.0 + nrm(ks[8], (DEPTH_2, HEAD_DIM_2), 0.02),
        'k_norm_g': 1.0 + nrm(ks[9], (DEPTH_2, HEAD_DIM_2), 0.02),
        'w_attn_out': nrm(ks[10], (DEPTH_2, Q_DIM, D_MODEL), Q_DIM ** -0.5),
        'conv_dw_w': nrm(ks[11], (DEPTH_2, CONV_WIDTH_2, CONV_DIM), CONV_WIDTH_2 ** -0.5),
        'conv_dw_b': nrm(ks[12], (DEPTH_2, CONV_DIM), 0.02),
        'conv_ln_g': 1.0 + nrm(ks[13], (DEPTH_2, CONV_DIM), 0.02),
        'conv_ln_b': nrm(ks[14], (DEPTH_2, CONV_DIM), 0.02),
        'w_conv_out': nrm(ks[15], (DEPTH_2, CONV_DIM, D_MODEL), CONV_DIM ** -0.5),
        'w_out': nrm(ks[16], (DEPTH_2, D_MODEL, D_MODEL), D_MODEL ** -0.5),
        'norm2_g': 1.0 + nrm(ks[17], (DEPTH_2, D_MODEL), 0.02),
        'w_up': nrm(ks[18], (DEPTH_2, D_MODEL, 2 * FFN_DIM), D_MODEL ** -0.5),
        'ffn_dw_w': nrm(ks[19], (DEPTH_2, FFN_CONV_WIDTH, FFN_DIM), FFN_CONV_WIDTH ** -0.5),
        'ffn_dw_b': nrm(ks[20], (DEPTH_2, FFN_DIM), 0.02),
        'w_down': nrm(ks[21], (DEPTH_2, FFN_DIM, D_MODEL), FFN_DIM ** -0.5),
        'final_g': 1.0 + nrm(ks[22], (D_MODEL,), 0.02),
    }

def second_block(x, c, ctx, c_ctx, w_mod, b_mod, norm1_g, w_in, q_norm_g, k_norm_g, w_attn_out,
              conv_dw_w, conv_dw_b, conv_ln_g, conv_ln_b, w_conv_out, w_out, norm2_g,
              w_up, ffn_dw_w, ffn_dw_b, w_down, final_g):
    B, L, _ = x.shape
    rows = L // GRID_W
    cos, sin = axial_rope(rows)
    for i in range(DEPTH_2):
        sh1, sc1, g1, sh2, sc2, g2 = modulation(c, w_mod[i], b_mod[i])
        csh1, csc1, cg1, csh2, csc2, cg2 = modulation(c_ctx[None], w_mod[i], b_mod[i])

        hx = modulate(rms_norm(x, norm1_g[i]), sh1, sc1)
        hc = modulate(rms_norm(ctx, norm1_g[i]), csh1, csc1)
        qx, kx, vx, ux, gx = project(hx, w_in[i], q_norm_g[i], k_norm_g[i])
        qx = apply_rope(qx, cos, sin)
        kx = apply_rope(kx, cos, sin)
        last = i == DEPTH_2 - 1
        if last:
            kc, vc = context_kv(hc, w_in[i], k_norm_g[i])
        else:
            qc, kc, vc, uc, gc = project(hc, w_in[i], q_norm_g[i], k_norm_g[i])
        attn_x = block_attention(qx, jnp.concatenate([kc, kx], axis=1), jnp.concatenate([vc, vx], axis=1))
        mix_x = merge_branches(attn_x, ux, gx, w_attn_out[i], conv_dw_w[i], conv_dw_b[i],
                               conv_ln_g[i], conv_ln_b[i], w_conv_out[i], w_out[i])
        x = x + g1 * mix_x
        hx2 = modulate(rms_norm(x, norm2_g[i]), sh2, sc2)
        x = x + g2 * conv_glu_ffn(hx2, w_up[i], ffn_dw_w[i], ffn_dw_b[i], w_down[i])

        if not last:
            attn_c = block_attention(qc, kc, vc)
            mix_c = merge_branches(attn_c, uc, gc, w_attn_out[i], conv_dw_w[i], conv_dw_b[i],
                                   conv_ln_g[i], conv_ln_b[i], w_conv_out[i], w_out[i])
            ctx = ctx + cg1 * mix_c
            hc2 = modulate(rms_norm(ctx, norm2_g[i]), csh2, csc2)
            ctx = ctx + cg2 * conv_glu_ffn(hc2, w_up[i], ffn_dw_w[i], ffn_dw_b[i], w_down[i])
    return rms_norm(x, final_g)


def setup_inputs(seed=0):
    out = dict(first_inputs(seed))
    for name, value in second_inputs(seed + 1).items():
        if name != "x":
            out[name + "_2"] = value
    return out


def reference(
    x, p, positions, mix_norm, ffn_norm, ffn_w_up, ffn_conv_w, ffn_conv_b, ffn_w_down, ple_norm,
    ple_w_gate, ple_w_proj, hy_w_in, hy_q_norm, hy_k_norm, hy_sinks, hy_conv_w, hy_w_out,
    gla_w_in, gla_w_gate_up, gla_gate_bias, gla_o_norm, gla_w_out, c_2, ctx_2, c_ctx_2, w_mod_2,
    b_mod_2, norm1_g_2, w_in_2, q_norm_g_2, k_norm_g_2, w_attn_out_2, conv_dw_w_2, conv_dw_b_2,
    conv_ln_g_2, conv_ln_b_2, w_conv_out_2, w_out_2, norm2_g_2, w_up_2, ffn_dw_w_2, ffn_dw_b_2,
    w_down_2, final_g_2,
):
    x = first_block(
        x, p, positions, mix_norm, ffn_norm, ffn_w_up, ffn_conv_w, ffn_conv_b, ffn_w_down,
        ple_norm, ple_w_gate, ple_w_proj, hy_w_in, hy_q_norm, hy_k_norm, hy_sinks, hy_conv_w,
        hy_w_out, gla_w_in, gla_w_gate_up, gla_gate_bias, gla_o_norm, gla_w_out,
    )
    return second_block(
        x, c_2, ctx_2, c_ctx_2, w_mod_2, b_mod_2, norm1_g_2, w_in_2, q_norm_g_2, k_norm_g_2,
        w_attn_out_2, conv_dw_w_2, conv_dw_b_2, conv_ln_g_2, conv_ln_b_2, w_conv_out_2, w_out_2,
        norm2_g_2, w_up_2, ffn_dw_w_2, ffn_dw_b_2, w_down_2, final_g_2,
    )


_drawn_inputs = setup_inputs


def setup_inputs(seed=0):
    import zlib

    import numpy as np

    out = dict(_drawn_inputs(seed))
    spreads = {}
    factors = {'ffn_conv_b': 3.039,
     'ple_norm': 5.294,
     'hy_q_norm': 8.0,
     'hy_k_norm': 8.0,
     'hy_sinks': 6.737,
     'gla_gate_bias': 3.573,
     'gla_o_norm': 3.01,
     'ctx_2': 8.0,
     'c_ctx_2': 4.755,
     'b_mod_2': 5.035,
     'norm1_g_2': 8.0,
     'q_norm_g_2': 8.0,
     'k_norm_g_2': 8.0,
     'conv_dw_b_2': 33.122,
     'conv_ln_g_2': 52.065,
     'conv_ln_b_2': 50.977,
     'norm2_g_2': 8.0,
     'ffn_dw_b_2': 23.77,
     'final_g_2': 9.025}
    for name, (base, spread) in spreads.items():
        noise = np.random.default_rng([zlib.crc32(name.encode()), seed]).standard_normal(out[name].shape)
        drawn = base * np.exp(spread * noise) if base else spread * noise
        out[name] = __import__('jax').numpy.asarray(drawn.astype(out[name].dtype))
    for name, factor in factors.items():
        out[name] = (out[name] * factor).astype(out[name].dtype)
    return out
```

```python
from contextlib import ExitStack

import numpy as np

import concourse.bass as bass
from concourse import mybir
from concourse.alu_op_type import AluOpType as ALU

ACT = mybir.ActivationFunctionType
F32 = mybir.dt.float32
F32R = mybir.dt.float32r
I32 = mybir.dt.int32
AX_X = mybir.AxisListType.X

P = 128
S = 256
NT = S // P
D = 1024
KC = D // P
FF = 2816
FC = FF // P
FP = FC // 2
TILE = 2048
SLOTS = 3
EPS = 1e-6
NEG = -1e30
TWO_PI = 2.0 * np.pi
PI_IN = float(np.nextafter(np.float32(np.pi), np.float32(0)))
_two_pi = [6.28125, 0.0019350051879882812]
TURN_PARTS = _two_pi + [float(TWO_PI - sum(_two_pi))]
ROUND = 12582912.0

HY_Q, HY_KV, HY_CC, HY_CX, HY_CB, HY_OUT = 0, 2, 3, 5, 7, 9
FFN0 = 13
FFN_TILES = 3 * FP
PLE0 = FFN0 + FFN_TILES
GLA = PLE0 + 5
GLA_OUT = GLA + 12
FFN1 = GLA + 16
PLE1 = FFN1 + FFN_TILES
MIX = PLE1 + 5
MIX_AO, MIX_CO, MIX_OUT = MIX + 18, MIX + 22, MIX + 24
FFN2 = MIX + 28
TILES = FFN2 + FFN_TILES
MOD_TILES = 24
MOD_BOTH = 8
MOD_HY, MOD_FFN0, MOD_FFN1 = {HY_KV + 3: 0, HY_OUT: 1, HY_OUT + 3: 2}, 3, 14
MOD_OUT = 48

PARAMS = {}
_at = 0
for _name, _width in [
    ("mix_norm0", 8), ("mix_norm1", 8), ("ffn_norm0", 8), ("ffn_norm1", 8), ("ple_norm0", 8), ("ple_norm1", 8),
    ("conv0", 4 * 2 * FC), ("conv1", 4 * 2 * FC), ("conv2", 4 * FC), ("hy_q", 1), ("hy_k", 1), ("sinks", 8),
    ("hy_conv", 12), ("gate_bias", 4), ("o_norm", 2), ("b_mod", MOD_OUT), ("norm1", 8), ("norm2", 8),
    ("q_g", 1), ("k_g", 1), ("dw", 31 * 4), ("dw_b", 4), ("ln_g", 4), ("ln_b", 4), ("final", 8), ("c", 16),
    ("glr_w", 8 * 16),
]:
    PARAMS[_name] = (_at, _width)
    _at += _width
N_PARAMS = _at

CONSTS = {}
_at = 0
for _name, _width in [
    ("ones", 128), ("inv_freq", 1), ("eps", 1), ("one", 1), ("ones_head", 128), ("eye", 128), ("rope_half", 128),
    ("rope_pair", 128), ("window", 256), ("levels", 8 * 128), ("cos", 256), ("sin", 256),
]:
    CONSTS[_name] = (_at, _width)
    _at += _width
N_CONSTS = _at
EARLY_CONSTS = CONSTS["levels"][0]


HY_SCALE = 64.0 ** -0.5
MIX_SCALE = 128.0 ** -0.5
HY_UNITS = {5: (0, 1), 6: (2, 3), 7: (4, 5), 8: (6, 7)}
MIX_UNITS = {MIX + 9: (0, 1), MIX + 11: (2, 3), MIX + 12: (4, 5, 6), MIX + 13: (7, 8), MIX + 14: (9, 10),
             MIX + 15: (11, 12), MIX + 16: (13, 14), MIX + 17: (15, 16, 17)}
HEAD_STEPS = {2: 0, 3: 1, 8: 2, 9: 3, 10: 4, 11: 5}
DVE_CONV = 2


class Tally:

    def __init__(self):
        self.count, self.per, self.turn = {}, {}, None

    def take(self, sem, k=1):
        self.count[sem.name] = self.count.get(sem.name, 0) + k
        return self.now(sem)

    def now(self, sem, back=0):
        n = self.count.get(sem.name, 0) - back
        per = self.per.get(sem.name, 0)
        return n if self.turn is None or not per else self.turn * per + n

    def loop(self, turn, per):
        self.turn, self.per, self.start = turn, {s.name: k for s, k in per.items()}, dict(self.count)

    def end(self, turns):
        for name, n in self.count.items():
            each = n - self.start.get(name, 0)
            assert each == self.per.get(name, 0), (name, each)
            self.count[name] = n + each * (turns - 1)
        self.turn, self.per = None, {}


def program(nc, stream, mod_stream, params_d, consts_d, up_d, x_d, p_d, ctx_d, pos_d, out_d):
    ctx = ExitStack()
    with ctx:
        place = [(nc.sbuf_base + 63) // 64 * 64]

        def sb(name, shape, dt=F32, at=None):
            size = 4 * int(np.prod(shape[1:]))
            if at is None:
                at = place[0]
                place[0] += (size + 31) // 32 * 32
            return nc.alloc_sbuf_tensor_at(name, shape, dt, offset=at)[...]

        def sem(name):
            return ctx.enter_context(nc.semaphore(name))

        landing = [sb(f"landing{i}", [P, TILE]) for i in range(SLOTS)]
        w_hi = [sb(f"w_hi{i}", [P, TILE], F32R) for i in range(SLOTS)]
        w_lo = [sb(f"w_lo{i}", [P, TILE], F32R) for i in range(SLOTS)]
        x = sb("x", [P, KC, S])
        nrm_at = place[0]
        nrm = sb("nrm", [P, KC, S])
        a_hi = sb("a_hi", [P, KC, S], F32R)
        a_lo = sb("a_lo", [P, KC, S], F32R)
        h_hi = sb("h_hi", [P, 2, S], F32R)
        h_lo = sb("h_lo", [P, 2, S], F32R)
        rstd = sb("rstd", [P, S])
        ffn_at = place[0]
        gate_c = sb("gate_c", [P, 2, S])
        up_c = sb("up_c", [P, 2, S])
        gelu_o = sb("gelu_o", [P, 2, S])
        hidden = sb("hidden", [P, 2, S])
        par = sb("par", [P, N_PARAMS])
        con = sb("con", [P, N_CONSTS])
        up_w = sb("up_w", [16, 512])
        mod = sb("mod", [P, MOD_OUT, 2])
        mod_sum = sb("mod_sum", [P, 2, 256])
        silu_c = sb("silu_c", [P, KC, 2])
        scale1 = sb("scale1", [P, 3, KC])
        raw_at = place[0]
        mod_raw = sb("mod_raw", [P, KC, 256])
        mod_mul = [sb(f"mod_mul{i}", [P, KC, 256]) for i in range(2)]
        arena = place[0]

        def region(start):
            at = [start]

            def take(name, shape, dt=F32):
                t = sb(name, shape, dt, at=at[0])
                at[0] += 4 * int(np.prod(shape[1:]))
                return t
            return take, at

        shared, at_s = region(arena)
        hsq = [shared(f"hsq{i}", [P, 2, S]) for i in range(2)]
        hrt = shared("hrt", [P, 2, S])
        hrot = shared("hrot", [P, 2, S])
        small = shared("small", [P, 2, 8, 2])
        mixer = at_s[0]
        over, _ = region(ffn_at)
        e_sb = [over(f"e_sb{i}", [P, 2, S]) for i in range(2)]
        pt_sb = [over(f"pt_sb{i}", [P, 4, P]) for i in range(2)]

        hy, at_h = region(mixer)
        s_sb = [hy(f"s_sb{i}", [P, 2, S]) for i in range(2)]
        hy_q = hy("hy_q", [P, 4, S])
        hy_k = hy("hy_k", [P, S])
        hy_v = hy("hy_v", [P, NT, P])
        hy_cc = hy("hy_cc", [P, 4, S])
        hy_z = hy("hy_z", [P, 4, S])
        hy_y = hy("hy_y", [P, 4, S])
        hy_o = hy("hy_o", [P, 4, S])
        rope_cos = hy("rope_cos", [P, S])
        rope_sin = hy("rope_sin", [P, S])
        posf = hy("posf", [P, S])
        ang = hy("ang", [P, S])
        turns_of = hy("turns_of", [P, S])
        pos = hy("pos", [P, S], I32)

        gl, at_g = region(arena)
        gq = gl("gq", [P, 4, S])
        gk = gl("gk", [P, 4, S])
        gg = gl("gg", [P, 4, S])
        gv = gl("gv", [P, NT, D])
        gog = gl("gog", [P, KC, S])
        gs0 = gl("gs0", [P, 4, S])
        gs1 = gl("gs1", [P, 4, P])
        glr = gl("glr", [16, S])
        ones4 = gl("ones4", [P, S])
        qp_at = at_g[0]
        gqp = [gl(f"gqp{i}", [P, 4, S]) for i in range(2)]
        over, _ = region(ffn_at)
        gkp = [over(f"gkp{i}", [P, 4, S]) for i in range(2)]
        over, _ = region(qp_at)
        gz = over("gz", [P, 4, S])
        gzl = over("gzl", [P, 4, S])
        over, _ = region(qp_at)
        ort = over("ort", [P, 4, S])
        over, _ = region(ffn_at)
        on = [over(f"on{i}", [P, 2, S]) for i in range(4)]
        over, _ = region(nrm_at)
        osq = [over(f"osq{i}", [P, 2, S]) for i in range(4)]
        over, _ = region(nrm_at)
        dl = [over(f"dl{i}", [P, 4, S]) for i in range(2)]

        mx, at_m = region(mixer)
        mk = mx("mk", [P, 2, 512])
        mv = mx("mv", [P, 4, 256])
        p_sb = sb("p_sb", [P, 2, S], at=at_m[0] - 4 * 4 * 256)
        pad = 15
        o_hi = mx("o_hi", [P, KC, S], F32R)
        cx = sb("cx", [P, KC, S], at=at_m[0] - 4 * KC * S)
        o_lo = mx("o_lo", [P, KC, S], F32R)
        c_at = at_m[0]
        c_hi = mx("c_hi", [P, KC, S], F32R)
        c_lo = mx("c_lo", [P, KC, S], F32R)
        over, _ = region(raw_at)
        mg = over("mg", [P, 2 * KC, S])
        mtmp = [over(f"mtmp{i}", [P, S]) for i in range(2)]
        mh = over("mh", [P, 4, S + 2 * pad])
        over, _ = region(nrm_at)
        acc = over("acc", [P, 4, S])
        lsq = over("lsq", [P, 4, S])
        ma = sb("ma", [P, 4, S], at=ffn_at + 2 * 4 * 2 * S)
        over, _ = region(c_at)
        mq = over("mq", [P, KC, S])
        l_hi = over("l_hi", [P, 4, S], F32R)
        l_lo = over("l_lo", [P, 4, S], F32R)
        assert max(place[0], at_h[0], at_g[0], at_m[0]) <= nc.sbuf_usable_end, (
            place[0], at_h[0], at_g[0], at_m[0], nc.sbuf_usable_end)

        banks = [ctx.enter_context(nc.psum_tensor(f"bank{i}", [P, 2, S], F32))[...] for i in range(8)]
        G, U, M0, M1, D0 = 0, 1, 2, 3, 4

        def c_(name, a=0, w=None):
            at, width = CONSTS[name]
            return con[:, at + a:at + a + (width - a if w is None else w)]

        def p_(name, a=0, w=1):
            return par[:, PARAMS[name][0] + a:PARAMS[name][0] + a + w]

        x_in = sem("x_in")
        par_in = sem("par_in")
        con_in = sem("con_in")
        late_in = sem("late_in")
        pos_in = sem("pos_in")
        p_in = sem("p_in")
        ctx_in = sem("ctx_in")
        landed = [sem(f"landed{i}") for i in range(SLOTS)]
        hi_ready = sem("hi_ready")
        lo_ready = sem("lo_ready")
        tile_used = sem("tile_used")
        mod_landed = sem("mod_landed")
        mod_taken = sem("mod_taken")
        pool_half = sem("pool_half")
        mod_four = sem("mod_four")
        mod_two = sem("mod_two")
        mod_added = sem("mod_added")
        mod_done = sem("mod_done")
        silu_ready = sem("silu_ready")
        bank_free = [sem("g_free"), sem("u_free")]
        act_done = sem("act_done")
        dve_done = sem("dve_done")
        pool_done = sem("pool_done")
        d_ready = sem("d_ready")
        res_ready = sem("res_ready")
        sq_ready = sem("sq_ready")
        ss_ready = sem("ss_ready")
        rt_ready = sem("rt_ready")
        nf_ready = sem("nf_ready")
        nhi_ready = sem("nhi_ready")
        n_ready = sem("n_ready")
        conv_base = sem("conv_base")
        gelu_ready = sem("gelu_ready")
        hidden_ready = sem("hidden_ready")
        hhi_ready = sem("hhi_ready")
        h_ready = sem("h_ready")
        y_hi_ready = sem("y_hi_ready")
        y_ready = sem("y_ready")
        hsq_ready = sem("hsq_ready")
        hss_ready = sem("hss_ready")
        hrt_ready = sem("hrt_ready")
        hn_ready = sem("hn_ready")
        hrot_ready = sem("hrot_ready")
        hrot_used = sem("hrot_used")
        rope_ready = sem("rope_ready")
        angle_ready = sem("angle_ready")
        table_ready = sem("table_ready")
        att_s = sem("att_s")
        att_half = sem("att_half")
        att_masked = sem("att_masked")
        att_m = sem("att_m")
        att_e = sem("att_e")
        att_p = sem("att_p")
        att_t = sem("att_t")
        att_pt = sem("att_pt")
        att_o = sem("att_o")
        glr_ready = sem("glr_ready")
        glr_copied = sem("glr_copied")
        gz_ready = sem("gz_ready")
        gz_read = sem("gz_read")
        ln_ready = sem("ln_ready")
        gg_ready = sem("gg_ready")
        dl_ready = sem("dl_ready")
        ee_ready = sem("ee_ready")
        qk_ready = sem("qk_ready")
        lev_ready = sem("lev_ready")
        lev_used = sem("lev_used")
        go_ready = sem("go_ready")
        osq_ready = sem("osq_ready")
        oss_ready = sem("oss_ready")
        ort_ready = sem("ort_ready")
        on_ready = sem("on_ready")
        hy_o_ready = sem("hy_o_ready")
        mh_ready = sem("mh_ready")
        pool_conv = sem("pool_conv")
        conv_ready = sem("conv_ready")
        lm_ready = sem("lm_ready")
        mu_ready = sem("mu_ready")
        cen_ready = sem("cen_ready")
        lsq_ready = sem("lsq_ready")
        lv_ready = sem("lv_ready")
        lrt_ready = sem("lrt_ready")
        ln_n_ready = sem("ln_n_ready")
        silu_done = sem("silu_done")
        lhi_ready = sem("lhi_ready")
        l_ready = sem("l_ready")
        mixed = sem("mixed")
        out_ready = sem("out_ready")
        stored = sem("stored")

        def banks_of(n):
            for f in (FFN0, FFN1, FFN2):
                if f <= n < f + FFN_TILES:
                    t = n - f
                    if t < 2:
                        return [(G, U)[t]]
                    return [] if t == FFN_TILES - 1 or (t - 2) % 3 == 2 else [(G, U)[(t - 2) % 3]]
            if n in (PLE0, PLE1):
                return []
            if n in (MIX_CO, MIX_CO + 1):
                return [G, U]
            return [n % 2]

        def co_banks(n):
            return (G, U) if n == MIX_CO else (D0 + 1, D0 + 2)

        FFN_TURNS = FP - 2

        block = ctx.enter_context(nc.Block())

        @block.sync
        def _(sp):
            sp.dma_start(x, x_d).then_inc(x_in, 16)
            sp.dma_start(con[:, 0:EARLY_CONSTS], consts_d[:, 0:EARLY_CONSTS]).then_inc(con_in, 16)

            def load(n, turn=None):
                slot = n % SLOTS
                if n >= SLOTS:
                    sp.wait_ge(lo_ready, n - SLOTS + 1 if turn is None else turn * SLOTS + (n - SLOTS + 1))
                src = stream[n] if turn is None else stream[bass.ds(turn * SLOTS + n, 1)].rearrange("a p c -> (a p) c")
                sp.dma_start(landing[slot], src).then_inc(landed[slot], 16)

            def load_mod(m, turn=None):
                if not (turn is None and m == 0):
                    sp.wait_ge(mod_taken, m if turn is None else turn + m)
                src = (mod_stream[m] if turn is None else
                       mod_stream[bass.ds(turn + m, 1)].rearrange("a p c -> (a p) c"))
                sp.dma_start(mod_raw.rearrange("p a b -> p (a b)"), src).then_inc(mod_landed, 16)

            def load_ffn(first, m):
                for n in range(first, first + 5):
                    load(n)
                turns = FFN_TURNS
                with sp.Fori(0, turns, 1) as turn:
                    for j in range(SLOTS):
                        load(first + 5 + j, turn)
                    if m is not None:
                        load_mod(m, turn)
                load(first + FFN_TILES - 1)

            load(0)
            sp.dma_start(par, params_d).then_inc(par_in, 16)
            load(1)
            sp.dma_start(pos, pos_d).then_inc(pos_in, 16)
            load(2)
            load_mod(0)
            sp.dma_start(con[:, EARLY_CONSTS:], consts_d[:, EARLY_CONSTS:]).then_inc(late_in, 16)
            sp.dma_start(up_w, up_d).then_inc(late_in, 16)
            for n in range(3, FFN0):
                load(n)
                if n in (HY_CX, HY_OUT):
                    load_mod((HY_CX, HY_OUT).index(n) + 1)
            load_mod(MOD_FFN0)
            load_ffn(FFN0, MOD_FFN0 + 1)
            sp.wait_ge(tile_used, FFN0)
            sp.dma_start(p_sb, p_d[:, 0:2, :]).then_inc(p_in, 16)
            for n in range(PLE0, FFN1):
                load(n)
                if n == GLA + 3:
                    load_mod(MOD_FFN1 - 1)
            load_mod(MOD_FFN1)
            load_ffn(FFN1, MOD_FFN1 + 1)
            sp.dma_start(p_sb, p_d[:, 2:4, :]).then_inc(p_in, 16)
            sp.dma_start(cx, ctx_d).then_inc(ctx_in, 16)
            for n in range(PLE1, FFN2):
                load(n)
            load_ffn(FFN2, None)
            for j in range(4):
                sp.wait_ge(out_ready, 2 * (j + 1))
                sp.dma_start(out_d[:, 2 * j:2 * j + 2, :], nrm[:, 2 * j:2 * j + 2, :]).then_inc(stored, 16)
            sp.wait_ge(stored, 64)

        @block.scalar
        def _(act):
            t = Tally()

            def own(ins):
                ins.then_inc(act_done, 1)
                return t.take(act_done)

            def split_hi(n, turn=None):
                if n >= TILES:
                    return
                at = (lambda k, per: k) if turn is None else (lambda k, per: turn * per + k)
                act.wait_ge(landed[n % SLOTS], at(16 * (n // SLOTS + 1), 16))
                if n >= SLOTS:
                    act.wait_ge(tile_used, at(n - SLOTS + 1, SLOTS))
                nc.scalar.activation(w_hi[n % SLOTS], landing[n % SLOTS], ACT.Copy).then_inc(hi_ready, 1)

            def results(n, turn=None):
                act.wait_ge(tile_used, n + 1 if turn is None else turn * SLOTS + (n + 1))

            def freed(n):
                return [(bank_free[b], t.take(bank_free[b])) for b in banks_of(n)]

            def inverse_root(dst, src, scale, sem_):
                act.wait_ge(act_done, own(nc.scalar.activation(dst, src, ACT.Ln, bias=c_("eps"), scale=scale)))
                nc.scalar.activation(dst, dst, ACT.Exp, scale=-0.5).then_inc(sem_, 1)

            def norm_squares(src, ready):
                for j in range(4):
                    if ready:
                        act.wait_ge(*ready[j])
                    nc.scalar.activation(nrm[:, 2 * j:2 * j + 2, :], src[:, 2 * j:2 * j + 2, :],
                                         ACT.Square).then_inc(sq_ready, 1)

            def norm_root():
                act.wait_ge(ss_ready, t.take(ss_ready))
                inverse_root(rstd, banks[M0][:, 0, :], 1.0 / D, rt_ready)

            def norm_rest(hi=None, bias=None, chunks=range(KC)):
                if chunks[0] == 0:
                    norm_root()
                if hi is not None:
                    for k in chunks:
                        act.wait_ge(nf_ready, t.take(nf_ready))
                        if bias is None:
                            ins = nc.scalar.activation(hi[:, k, :], nrm[:, k, :], ACT.Copy)
                        else:
                            ins = nc.scalar.activation(hi[:, k, :], nrm[:, k, :], ACT.Identity, bias=bias(k))
                        ins.then_inc(nhi_ready, 1)

            def norm(src, ready, hi=None, bias=None):
                norm_squares(src, ready)
                norm_rest(hi, bias)

            def out_hi(dst, src, scale=1.0):
                nc.scalar.activation(dst, src, ACT.Copy, scale=scale).then_inc(y_hi_ready, 1)

            def ffn(first, conv, func, both):
                at = PARAMS[conv][0]
                tap = 2 if both else 1

                def base(bank, dst, pair, turn, up):
                    for j in range(2):
                        off = at + 4 * (FC * up + 2 * pair + j)
                        col = lambda k: (par[:, off + k:off + k + 1] if turn is None
                                         else par[:, bass.ds(turn * 8 + (off + k), 1)])
                        nc.scalar.activation(dst[:, j, :], banks[bank][:, j, :], ACT.Identity, bias=col(3),
                                             scale=col(tap)).then_inc(conv_base, 1)

                def gate(pair, n, turn):
                    results(n, turn)
                    base(G, gate_c, pair, turn, 0)
                    t.take(bank_free[G])

                def up(pair, n, turn):
                    results(n, turn)
                    if both:
                        base(U, up_c, pair, turn, 1)
                        t.take(bank_free[U])
                    else:
                        nc.scalar.activation(up_c, banks[U], ACT.Copy).then_inc(bank_free[U], 1)
                        t.take(bank_free[U])
                    act.wait_ge(bank_free[G], t.now(bank_free[G]))
                    nc.scalar.activation(gelu_o, gate_c, func).then_inc(gelu_ready, 1)

                def hidden_hi(n, turn, dst=h_hi):
                    act.wait_ge(hidden_ready, t.take(hidden_ready))
                    results(n, turn)
                    nc.scalar.activation(dst, hidden, ACT.Copy).then_inc(hhi_ready, 1)

                def pair_steps(pair, n, turn=None):
                    split_hi(n + 2, turn)
                    hidden_hi(n - 1, turn)
                    split_hi(n + 3, turn)
                    gate(pair, n, turn)
                    if pair < FP - 1:
                        split_hi(n + 4, turn)
                    up(pair, n + 1, turn)

                split_hi(first + 2)
                split_hi(first + 3)
                gate(0, first, None)
                up(0, first + 1, None)
                pair_steps(1, first + 2)
                turns = FFN_TURNS - 1
                with act.Fori(0, turns, 1) as turn:
                    t.loop(turn, {hidden_ready: 1, bank_free[G]: 1, bank_free[U]: 1})
                    pair_steps(2, first + 5, turn)
                t.end(turns)
                for pair in range(2 + turns, FP):
                    pair_steps(pair, first + 3 * pair - 1)
                hidden_hi(first + FFN_TILES - 3, None, a_hi[:, 0:2, :])
                split_hi(first + FFN_TILES)
                split_hi(first + FFN_TILES + 1)
                return [(res_ready, t.take(res_ready)) for j in range(4)]

            def ple(first, layer, ready, after=None):
                act.wait_ge(p_in, 16 * (layer + 1))
                results(first - 1)
                nc.scalar.activation(h_hi, p_sb, ACT.Copy).then_inc(hhi_ready, 1)
                norm(x, ready, a_hi)
                split_hi(first + 2)
                tokens = []
                for c in range(4):
                    n = first + 1 + c
                    if c:
                        sigmoid(n - 1, c - 1, tokens)
                    split_hi(n + 2)
                    if after:
                        after(c)
                sigmoid(first + 4, 3, tokens)
                return tokens

            def sigmoid(n, c, tokens):
                results(n)
                if c >= 2:
                    act.wait_ge(*tokens[c - 2])
                freed(n)
                nc.scalar.activation((gate_c, up_c)[c % 2], banks[n % 2], ACT.Sigmoid).then_inc(bank_free[n % 2], 1)
                tokens.append((res_ready, t.take(res_ready)))

            def head_square(group, src):
                nc.scalar.activation(hsq[group % 2][:, 0:src.shape[1], :], src, ACT.Square).then_inc(hsq_ready, 1)

            def head_root(width, scale):
                act.wait_ge(hss_ready, t.take(hss_ready))
                if t.now(hn_ready):
                    act.wait_ge(hn_ready, t.now(hn_ready))
                t.take(hn_ready)
                inverse_root(hrt[:, 0:width, :], banks[M0][:, 0:width, :], scale, hrt_ready)

            def attend_copy(u):
                act.wait_ge(att_t, t.take(att_t))
                if u >= 2:
                    act.wait_ge(att_o, t.take(att_o))
                nc.scalar.activation(pt_sb[u % 2], banks[D0 + 2 + u % 2].rearrange("p a (b c) -> p (a b) c", c=P),
                                     ACT.Copy).then_inc(att_pt, 1)

            def attend_copy_part(u, blocks):
                act.wait_ge(att_t, t.take(att_t))
                if u >= 2:
                    act.wait_ge(att_o, t.take(att_o))
                nc.scalar.activation(pt_sb[u % 2][:, 0:blocks, :],
                                     banks[D0 + 2 + u % 2].rearrange("p a (b c) -> p (a b) c", c=P)[:, 0:blocks, :],
                                     ACT.Copy).then_inc(att_pt, 1)

            act.wait_ge(x_in, 16)
            act.wait_ge(con_in, 16)
            norm_squares(x, None)
            split_hi(0)
            norm_rest(a_hi)
            split_hi(1)
            act.wait_ge(par_in, 16)
            nc.scalar.activation(silu_c, p_("c", 0, 16).rearrange("p (k c) -> p k c", c=2),
                                 ACT.Silu).then_inc(silu_ready, 1)
            act.wait_ge(angle_ready, 2)
            nc.scalar.activation(rope_sin, rope_sin, ACT.Sin).then_inc(table_ready, 1)
            nc.scalar.activation(rope_cos, rope_cos, ACT.Sin).then_inc(table_ready, 1)

            def hy_unit(i):
                if i in (6, 10):
                    tt = (i - 6) // 4
                    act.wait_ge(att_o, 4 * (tt + 1))
                    nc.scalar.activation(hy_o[:, :, P * tt:P * tt + P],
                                         banks[M0].rearrange("p a (b c) -> p (a b) c", c=P),
                                         ACT.Copy).then_inc(hy_o_ready, 1)
                if 1 <= i < 9:
                    attend_copy_part(i - 1, 2 * (1 + (i - 1) // 4))
                if i < 8:
                    tt = i // 4
                    w = P * (tt + 1)
                    act.wait_ge(att_m, t.take(att_m))
                    for g in range(2):
                        nc.scalar.activation(e_sb[i % 2][:, g, 0:w], s_sb[i % 2][:, g, 0:w], ACT.Exp,
                                             bias=small[:, i % 2, 1, g:g + 1], scale=HY_SCALE,
                                             accum_out=small[:, i % 2, 2, g:g + 1])
                    nc.scalar.activation(small[:, i % 2, 5, :], small[:, i % 2, 4, :], ACT.Exp).then_inc(att_e, 1)

            def hy_post(n):
                results(n)
                bank = banks[n % 2]
                freed(n)
                if n < HY_KV:
                    head_square(n, bank)
                    nc.scalar.activation(hy_q[:, 2 * n:2 * n + 2, :], bank, ACT.Copy).then_inc(bank_free[n % 2], 1)
                elif n == HY_KV:
                    head_square(2, bank[:, 0:1, :])
                    nc.scalar.activation(hy_k, bank[:, 0, :], ACT.Copy)
                    nc.scalar.activation(hy_v, bank[:, 1, :].rearrange("p (a b) -> p a b", a=NT),
                                         ACT.Copy).then_inc(bank_free[n % 2], 1)
                elif n < HY_CX:
                    j = n - HY_CC
                    nc.scalar.activation(hy_cc[:, 2 * j:2 * j + 2, :], bank, ACT.Copy).then_inc(bank_free[n % 2], 1)
                elif n < HY_CB:
                    j = n - HY_CX
                    act.wait_ge(bank_free[n % 2], t.now(bank_free[n % 2]))
                    for c in (2 * j, 2 * j + 1):
                        nc.scalar.activation(hy_y[:, c, :], hy_z[:, c, :], ACT.Copy,
                                             scale=p_("hy_conv", 3 * c + 2)).then_inc(conv_base, 1)

            cb_tokens = []
            for n in range(HY_OUT):
                split_hi(n + 2)
                if n:
                    hy_post(n - 1)
                    if n - 1 >= HY_CB:
                        cb_tokens.append((bank_free[(n - 1) % 2], t.now(bank_free[(n - 1) % 2])))
                if 2 <= n <= 4:
                    head_root(2 if n < 4 else 1, 1.0 / 64)
                for i in HY_UNITS.get(n, ()):
                    hy_unit(i)
            split_hi(HY_OUT + 2)
            hy_post(HY_OUT - 1)
            cb_tokens.append((bank_free[(HY_OUT - 1) % 2], t.now(bank_free[(HY_OUT - 1) % 2])))
            for j in range(2):
                act.wait_ge(*cb_tokens[j])
                out_hi(a_hi[:, 4 + 2 * j:6 + 2 * j, :], hy_y[:, 2 * j:2 * j + 2, :])
            for i in (8, 9, 10):
                hy_unit(i)
            t.take(att_o, 8 - t.now(att_o))
            for tt in range(NT):
                act.wait_ge(hy_o_ready, tt + 1)
                out_hi(a_hi[:, 0:4, P * tt:P * tt + P], hy_o[:, :, P * tt:P * tt + P])
            tokens = freed(HY_OUT)
            for n in range(HY_OUT + 1, FFN0):
                split_hi(n + 2)
                tokens += freed(n)
            norm(x, tokens, a_hi)
            tokens = ffn(FFN0, "conv0", ACT.Gelu, True)
            tokens = ple(PLE0, 0, tokens)

            norm(x, tokens, a_hi)

            def decay(level):
                act.wait_ge(dl_ready, t.take(dl_ready))
                d = dl[level % 2]
                act.wait_ge(act_done, own(nc.scalar.activation(d, d, ACT.Abs)))
                nc.scalar.activation(d, d, ACT.Exp, scale=-1.0 / 16).then_inc(ee_ready, 1)

            def gla_post(n):
                results(n)
                freed(n)
                b = n % 2
                j = n - GLA
                if j < 2:
                    ins = nc.scalar.activation(gq[:, 2 * j:2 * j + 2, :], banks[b], ACT.Copy, scale=float(P) ** -0.5)
                elif j < 4:
                    ins = nc.scalar.activation(gk[:, 2 * j - 4:2 * j - 2, :], banks[b], ACT.Copy)
                elif j < 8:
                    ins = nc.scalar.activation(gv[:, :, 256 * (j - 4):256 * (j - 3)], banks[b], ACT.Copy)
                else:
                    ins = nc.scalar.activation(gog[:, 2 * j - 16:2 * j - 14, :], banks[b], ACT.Silu)
                ins.then_inc(bank_free[b], 1)

            for n in range(GLA, GLA_OUT):
                split_hi(n + 2)
                if n == GLA + 1:
                    act.wait_ge(glr_ready, 1)
                    nc.scalar.activation(glr, banks[M0][0:16, 0, :], ACT.Copy).then_inc(glr_copied, 1)
                if n > GLA:
                    gla_post(n - 1)
                if n == GLA + 2:
                    act.wait_ge(gz_read, 1)
                    act.wait_ge(act_done, own(nc.scalar.activation(gzl, gz, ACT.Abs)))
                    act.wait_ge(act_done, own(nc.scalar.activation(gzl, gzl, ACT.Exp, scale=-1.0)))
                    nc.scalar.activation(gzl, gzl, ACT.Ln, bias=c_("one")).then_inc(ln_ready, 1)
                if GLA + 3 <= n < GLA + 11:
                    decay(n - GLA - 2)
            gla_post(GLA_OUT - 1)
            for h in range(4):
                act.wait_ge(go_ready, h + 1)
                nc.scalar.activation(osq[h], banks[D0 + h], ACT.Square).then_inc(osq_ready, 1)
            for j in range(2):
                act.wait_ge(oss_ready, j + 1)
                inverse_root(ort[:, 2 * j:2 * j + 2, :], banks[M0], 1.0 / 256, ort_ready)
            for h in range(4):
                act.wait_ge(on_ready, h + 1)
                out_hi(a_hi[:, 2 * h:2 * h + 2, :], on[h])
            tokens = []
            for n in range(GLA_OUT, FFN1):
                split_hi(n + 2)
                tokens += freed(n)
            norm(x, tokens, a_hi)
            tokens = ffn(FFN1, "conv1", ACT.Gelu, True)

            def context_norm(c):
                if c == 0:
                    act.wait_ge(ctx_in, 16)
                    act.wait_ge(n_ready, 6 * KC)
                    norm_squares(cx, None)
                norm_rest(c_hi, lambda k: mod[:, k, 1:2], range(2 * c, 2 * c + 2))

            tokens = ple(PLE1, 1, tokens, context_norm)

            act.wait_ge(n_ready, 7 * KC)
            norm(x, tokens, a_hi, lambda k: mod[:, k, 0:1])

            def mix_post(n):
                results(n)
                freed(n)
                j, b = n - MIX, n % 2
                if j == 0:
                    head_square(0, banks[b])
                    head_square(1, banks[D0 + 2])
                    nc.scalar.activation(mk[:, :, 0:S], banks[D0 + 2], ACT.Copy)
                    nc.scalar.activation(mk[:, :, S:2 * S], banks[b], ACT.Copy).then_inc(bank_free[b], 1)
                elif j == 1:
                    nc.scalar.activation(mv[:, 0:2, :], banks[D0 + 3], ACT.Copy)
                    nc.scalar.activation(mv[:, 2:4, :], banks[b], ACT.Copy).then_inc(bank_free[b], 1)
                elif j < 4:
                    nc.scalar.activation(ma[:, 2 * j - 4:2 * j - 2, :], banks[b], ACT.Copy,
                                         scale=0.5).then_inc(bank_free[b], 1)
                elif 6 <= j < 10:
                    head_square(j, banks[b])
                    nc.scalar.activation(mq[:, 2 * j - 12:2 * j - 10, :], banks[b], ACT.Copy).then_inc(bank_free[b], 1)
                elif j < 6:
                    nc.scalar.activation((gate_c, up_c)[j % 2], banks[b], ACT.Tanh, scale=0.5).then_inc(bank_free[b], 1)
                elif j < 18:
                    nc.scalar.activation(mg[:, 2 * j - 20:2 * j - 18, :], banks[b], ACT.Tanh,
                                         scale=0.5).then_inc(bank_free[b], 1)

            def mix_unit(i):
                if i >= 4 and i % 2 == 0:
                    h = (i - 4) // 2
                    act.wait_ge(att_o, 8 + 2 * (h + 1))
                    out_hi(o_hi[:, h, :], banks[M0 + h % 2][:, 0, :])
                if 1 <= i < 17:
                    attend_copy(i - 1)
                if i < 16:
                    act.wait_ge(att_m, t.take(att_m))
                    nc.scalar.activation(e_sb[i % 2], banks[D0 + i % 2], ACT.Exp, bias=small[:, i % 2, 1, 0:1],
                                         scale=MIX_SCALE, accum_out=small[:, i % 2, 2, 0:1]).then_inc(att_e, 1)

            def mix_hi(pair):
                for j in (pair, pair + 1):
                    act.wait_ge(mixed, t.take(mixed))
                    out_hi(a_hi[:, 2 * j:2 * j + 2, :], mg[:, KC + 2 * j:KC + 2 * j + 2, :], 0.5)

            for n in range(MIX, MIX_OUT):
                if n == MIX_CO + 1:
                    mix_hi(0)
                split_hi(n + 2)
                if n > MIX:
                    mix_post(n - 1)
                if n - MIX in HEAD_STEPS:
                    head_root(2, 1.0 / P)
                if n == MIX + 6:
                    act.wait_ge(mh_ready, 2)
                    for c in range(DVE_CONV):
                        nc.scalar.activation(acc[:, c, :], mh[:, c, 0:S], ACT.Identity, bias=p_("dw_b", c),
                                             scale=p_("dw", 31 * c)).then_inc(conv_base, 1)
                for i in MIX_UNITS.get(n, ()):
                    mix_unit(i)
                if n == MIX_AO:
                    mix_unit(18)
                    act.wait_ge(lm_ready, 1)
                    nc.scalar.activation(hrt[:, 0, :], banks[M0][:, 0, :], ACT.Copy, scale=1.0 / 512).then_inc(mu_ready, 1)
                    act.wait_ge(cen_ready, 1)
                    nc.scalar.activation(lsq, acc, ACT.Square).then_inc(lsq_ready, 1)
                if n == MIX_AO + 1:
                    act.wait_ge(lv_ready, 1)
                    inverse_root(hrt[:, 1, :], banks[D0][:, 0, :], 1.0 / 512, lrt_ready)
                    act.wait_ge(ln_n_ready, 1)
                    for c in range(4):
                        done = own(nc.scalar.activation(lsq[:, c, :], acc[:, c, :], ACT.Silu, bias=p_("ln_b", c),
                                                        scale=p_("ln_g", c)))
                    act.wait_ge(act_done, done)
                    nc.scalar.activation(l_hi, lsq, ACT.Copy).then_inc(lhi_ready, 1)
            results(MIX_OUT - 1)
            freed(MIX_OUT - 1)
            mix_hi(2)
            tokens = []
            for n in range(MIX_OUT, FFN2):
                split_hi(n + 2)
                tokens += freed(n)
            norm(x, tokens, a_hi, lambda k: mod[:, 24 + k, 0:1])
            tokens = ffn(FFN2, "conv2", ACT.Gelu_apprx_tanh, False)
            norm(x, tokens)

        @block.vector
        def _(dve):
            t = Tally()
            v = nc.vector

            def own(ins):
                ins.then_inc(dve_done, 1)
                return t.take(dve_done)

            def chain(ins):
                dve.wait_ge(dve_done, own(ins))

            def split_lo(n, turn=None):
                if n >= TILES:
                    return
                dve.wait_ge(hi_ready, n + 1 if turn is None else turn * SLOTS + (n + 1))
                k = n % SLOTS
                v.tensor_tensor(w_lo[k], landing[k], w_hi[k].bitcast(F32), ALU.subtract).then_inc(lo_ready, 1)

            def results(n, turn=None):
                dve.wait_ge(tile_used, n + 1 if turn is None else turn * SLOTS + (n + 1))

            def freed(n):
                return [(bank_free[b], t.take(bank_free[b])) for b in banks_of(n)]

            def norm(src, gain, hi=None, lo=None, bias=None, chunks=range(KC)):
                if chunks[0] == 0:
                    dve.wait_ge(rt_ready, t.take(rt_ready))
                end = chunks[-1] + 1
                for k in [*chunks, end]:
                    if k < end:
                        v.scalar_tensor_tensor(nrm[:, k, :], src[:, k, :], gain(k), rstd, ALU.mult,
                                               ALU.mult).then_inc(nf_ready if hi is not None else out_ready, 1)
                    if k > chunks[0] and hi is not None:
                        dve.wait_ge(nhi_ready, t.take(nhi_ready))
                        part = hi[:, k - 1, :].bitcast(F32)
                        if bias is None:
                            ins = v.tensor_tensor(lo[:, k - 1, :], nrm[:, k - 1, :], part, ALU.subtract)
                        else:
                            ins = v.scalar_tensor_tensor(lo[:, k - 1, :], nrm[:, k - 1, :], bias(k - 1), part,
                                                         ALU.add, ALU.subtract)
                        ins.then_inc(n_ready, 1)

            def residual(n, j):
                results(n)
                freed(n)
                v.tensor_tensor(x[:, 2 * j:2 * j + 2, :], x[:, 2 * j:2 * j + 2, :], banks[n % 2],
                                ALU.add).then_inc(bank_free[n % 2], 1)

            def out_lo(dst, src, hi):
                dve.wait_ge(y_hi_ready, t.take(y_hi_ready))
                v.tensor_tensor(dst, src, hi.bitcast(F32), ALU.subtract).then_inc(y_ready, 1)

            def ffn(first, conv, both, add):
                at = PARAMS[conv][0]

                def rest(bank, dst, pair, turn, up):
                    taps = ((1, 1, 0), (0, 2, 0)) if both else ((0, 1, 0), (2, 0, 1))
                    dve.wait_ge(conv_base, t.take(conv_base, 2))
                    done = []
                    for step, (tap, late, early) in enumerate(taps):
                        for j in range(2):
                            off = at + 4 * (FC * up + 2 * pair + j) + tap
                            w = par[:, off:off + 1] if turn is None else par[:, bass.ds(turn * 8 + off, 1)]
                            if step:
                                dve.wait_ge(dve_done, done[j])
                            out = dst[:, j, late:S - early]
                            ins = v.scalar_tensor_tensor(out, banks[bank][:, j, early:S - late], w, out,
                                                         ALU.mult, ALU.add)
                            if step and j:
                                ins.then_inc(bank_free[bank], 1)
                            else:
                                done.append(own(ins))

                def gate(pair, turn):
                    rest(G, gate_c, pair, turn, 0)
                    t.take(bank_free[G])

                def up(pair, turn):
                    if both:
                        rest(U, up_c, pair, turn, 1)
                    t.take(bank_free[U])
                    dve.wait_ge(bank_free[U], t.now(bank_free[U]))
                    dve.wait_ge(gelu_ready, t.take(gelu_ready))
                    v.tensor_tensor(hidden, gelu_o, up_c, ALU.mult).then_inc(hidden_ready, 1)

                def hidden_lo(dst=h_lo, high=h_hi):
                    dve.wait_ge(hhi_ready, t.take(hhi_ready))
                    v.tensor_tensor(dst, hidden, high.bitcast(F32), ALU.subtract).then_inc(h_ready, 1)

                def pair_steps(pair, n, turn=None):
                    split_lo(n + 2, turn)
                    hidden_lo()
                    split_lo(n + 3, turn)
                    gate(pair, turn)
                    if pair < FP - 1:
                        split_lo(n + 4, turn)
                    up(pair, turn)

                split_lo(first + 2)
                split_lo(first + 3)
                gate(0, None)
                up(0, None)
                pair_steps(1, first + 2)
                turns = FFN_TURNS - 1
                with dve.Fori(0, turns, 1) as turn:
                    t.loop(turn, {dve_done: 6 if both else 3, conv_base: 4 if both else 2, bank_free[G]: 1,
                                  bank_free[U]: 1, gelu_ready: 1, hhi_ready: 1})
                    pair_steps(2, first + 5, turn)
                t.end(turns)
                for pair in range(2 + turns, FP):
                    pair_steps(pair, first + 3 * pair - 1)
                hidden_lo(a_lo[:, 0:2, :], a_hi[:, 0:2, :])
                split_lo(first + FFN_TILES)
                split_lo(first + FFN_TILES + 1)
                for j in range(4):
                    dve.wait_ge(d_ready, t.take(d_ready))
                    add(j)

            def add_plain(j):
                v.tensor_tensor(x[:, 2 * j:2 * j + 2, :], x[:, 2 * j:2 * j + 2, :], banks[D0 + j],
                                ALU.add).then_inc(res_ready, 1)
                t.take(res_ready)

            def add_gated(j):
                for c in range(2):
                    k = 2 * j + c
                    ins = v.scalar_tensor_tensor(x[:, k, :], banks[D0 + j][:, c, :], mod[:, 40 + k, 0:1],
                                                 x[:, k, :], ALU.mult, ALU.add)
                    if c:
                        ins.then_inc(res_ready, 1)
                    else:
                        own(ins)
                t.take(res_ready)

            def ple(first, layer, after=None):
                dve.wait_ge(hhi_ready, t.take(hhi_ready))
                v.tensor_tensor(h_lo, p_sb, h_hi.bitcast(F32),
                                ALU.subtract).then_inc(h_ready, 1)
                norm(x, lambda k: p_(f"ple_norm{layer}", k), a_hi, a_lo)
                split_lo(first + 2)
                for c in range(4):
                    n = first + 1 + c
                    if c:
                        gated(n - 1, c - 1)
                    split_lo(n + 2)
                    if after:
                        after(c)
                gated(first + 4, 3)

            def gated(n, c):
                sig = (gate_c, up_c)[c % 2]
                freed(n)
                dve.wait_ge(bank_free[n % 2], t.now(bank_free[n % 2]))
                chain(v.tensor_tensor(sig, sig, banks[D0 + c], ALU.mult))
                v.tensor_tensor(x[:, 2 * c:2 * c + 2, :], x[:, 2 * c:2 * c + 2, :], sig,
                                ALU.add).then_inc(res_ready, 1)
                t.take(res_ready)

            def head_norm(raw, gain):
                c = raw.shape[1]
                dve.wait_ge(hrt_ready, t.take(hrt_ready))
                v.scalar_tensor_tensor(raw, raw, gain, hrt[:, 0:c, :], ALU.mult, ALU.mult).then_inc(hn_ready, 1)

            def rotate(raw, cos, sin):
                c = raw.shape[1]
                dve.wait_ge(hrot_ready, t.take(hrot_ready))
                r = hrot[:, 0:c, :]
                v.tensor_tensor(r, banks[D0][:, 0:c, :], sin.unsqueeze(1).broadcast_to([P, c, S]),
                                ALU.mult).then_inc(hrot_used, 1)
                t.take(hrot_used)
                chain(v.tensor_tensor(raw, raw, cos.unsqueeze(1).broadcast_to([P, c, S]), ALU.mult))
                dve.wait_ge(hrot_used, t.now(hrot_used))
                v.tensor_tensor(raw, raw, r, ALU.add).then_inc(rope_ready, 1)

            split_lo(0)
            dve.wait_ge(x_in, 16)
            dve.wait_ge(par_in, 16)
            norm(x, lambda k: p_("mix_norm0", k), a_hi, a_lo)
            split_lo(1)
            dve.wait_ge(pos_in, 16)
            chain(v.tensor_copy(posf, pos))
            chain(v.tensor_scalar(ang, posf, c_("inv_freq"), None, ALU.mult))
            chain(v.tensor_scalar(turns_of, ang, 1.0 / TWO_PI, ROUND, ALU.mult, ALU.add))
            chain(v.tensor_scalar(turns_of, turns_of, ROUND, None, ALU.subtract))
            for part in TURN_PARTS:
                chain(v.scalar_tensor_tensor(ang, turns_of, -part, ang, ALU.mult, ALU.add))
            v.tensor_scalar(rope_sin, ang, PI_IN, -PI_IN, ALU.min, ALU.max).then_inc(angle_ready, 1)
            chain(v.tensor_scalar(ang, ang, float(np.float32(np.pi / 2)), None, ALU.add))
            chain(v.tensor_scalar(turns_of, ang, PI_IN, -float(np.float32(TWO_PI)), ALU.is_gt, ALU.mult))
            chain(v.tensor_tensor(ang, ang, turns_of, ALU.add))
            v.tensor_scalar(rope_cos, ang, PI_IN, -PI_IN, ALU.min, ALU.max).then_inc(angle_ready, 1)

            hy_raw = [hy_q[:, 0:2, :], hy_q[:, 2:4, :], hy_k.unsqueeze(1)]
            hy_gain = [p_("hy_q"), p_("hy_q"), p_("hy_k")]

            divided = set()

            def hy_divide(u):
                if 0 <= u < 8 and u not in divided:
                    divided.add(u)
                    w = P * (u // 4 + 1)
                    sm = small[:, u % 2]
                    dve.wait_ge(att_e, t.take(att_e))
                    chain(v.tensor_tensor(sm[:, 6, :], sm[:, 2, :], sm[:, 5, :], ALU.add))
                    chain(v.reciprocal(sm[:, 3, :], sm[:, 6, :]))
                    for g in range(2):
                        e = e_sb[u % 2][:, g, 0:w]
                        ins = v.tensor_scalar(e, e, sm[:, 3, g:g + 1], None, ALU.mult)
                        if g:
                            ins.then_inc(att_p, 1)
                        else:
                            own(ins)

            def hy_unit(i):
                hy_divide(i - 1)
                if i < 8:
                    tt, c = i // 4, i % 4
                    w = P * (tt + 1)
                    s, sm = s_sb[i % 2][:, :, 0:w], small[:, i % 2]
                    dve.wait_ge(att_s, t.take(att_s))
                    v.tensor_tensor(s, banks[D0 + i % 2][:, :, 0:w],
                                    c_("window", 2 * P - w, w).unsqueeze(1).broadcast_to([P, 2, w]),
                                    ALU.add).then_inc(att_masked, 1)
                    dve.wait_ge(att_masked, t.take(att_masked))
                    chain(v.tensor_reduce(sm[:, 0, :], s, AX_X, ALU.max))
                    sinks = p_("sinks", 2 * c, 2)
                    chain(v.scalar_tensor_tensor(sm[:, 0, :], sm[:, 0, :], HY_SCALE, sinks, ALU.mult, ALU.max))
                    chain(v.tensor_scalar(sm[:, 1, :], sm[:, 0, :], -1.0, None, ALU.mult))
                    v.tensor_tensor(sm[:, 4, :], sinks, sm[:, 1, :], ALU.add).then_inc(att_m, 1)

            def hy_post(n):
                f = freed(n)
                b, bank = n % 2, banks[n % 2]
                if HY_CC <= n < HY_CX:
                    cc_tokens.extend(f)
                elif HY_CX <= n < HY_CB:
                    j = n - HY_CX
                    pair = slice(2 * j, 2 * j + 2)
                    results(n)
                    dve.wait_ge(*cc_tokens[j])
                    v.tensor_tensor(hy_z[:, pair, :], hy_cc[:, pair, :], bank, ALU.mult).then_inc(bank_free[b], 1)
                    dve.wait_ge(conv_base, t.take(conv_base, 2))
                    for back in (1, 2):
                        for c in (2 * j, 2 * j + 1):
                            if back == 2:
                                dve.wait_ge(dve_done, t.now(dve_done, 1))
                            out = hy_y[:, c, back:S]
                            own(v.scalar_tensor_tensor(out, hy_z[:, c, 0:S - back], p_("hy_conv", 3 * c + 2 - back),
                                                       out, ALU.mult, ALU.add))
                elif n >= HY_CB:
                    j = n - HY_CB
                    pair = slice(2 * j, 2 * j + 2)
                    results(n)
                    dve.wait_ge(dve_done, t.now(dve_done))
                    v.tensor_tensor(hy_y[:, pair, :], hy_y[:, pair, :], bank, ALU.mult).then_inc(bank_free[b], 1)

            cc_tokens = []
            for n in range(HY_OUT):
                split_lo(n + 2)
                if n:
                    hy_post(n - 1)
                if 3 <= n <= 5:
                    if n == 3:
                        dve.wait_ge(table_ready, 2)
                    rotate(hy_raw[n - 3], rope_cos, rope_sin)
                if 2 <= n <= 4:
                    head_norm(hy_raw[n - 2], hy_gain[n - 2])
                for i in HY_UNITS.get(n, ()):
                    hy_unit(i)
                if n in HY_UNITS:
                    hy_divide(HY_UNITS[n][-1])
            split_lo(HY_OUT + 2)
            hy_post(HY_OUT - 1)
            for j in range(2):
                k = slice(4 + 2 * j, 6 + 2 * j)
                out_lo(a_lo[:, k, :], hy_y[:, 2 * j:2 * j + 2, :], a_hi[:, k, :])
            for i in (8, 9, 10):
                hy_unit(i)
            for tt in range(NT):
                cols = slice(P * tt, P * tt + P)
                out_lo(a_lo[:, 0:4, cols], hy_o[:, :, cols], a_hi[:, 0:4, cols])
            for n in range(HY_OUT, FFN0):
                if n > HY_OUT:
                    split_lo(n + 2)
                if n > HY_OUT:
                    residual(n - 1, n - 1 - HY_OUT)
            residual(FFN0 - 1, 3)
            norm(x, lambda k: p_("ffn_norm0", k), a_hi, a_lo)
            ffn(FFN0, "conv0", True, add_plain)
            ple(PLE0, 0)

            norm(x, lambda k: p_("mix_norm1", k), a_hi, a_lo)
            chain(v.memset(ones4, 1.0))

            def distance(level):
                half = 1 << (level - 1)
                if level >= 3:
                    dve.wait_ge(qk_ready, level - 2)
                blocks = 4 * S // (2 * half)
                src = gg.rearrange("p a (b c) -> p (a b) c", c=2 * half)
                v.tensor_tensor(dl[level % 2].rearrange("p a (b c) -> p (a b) c", c=2 * half), src,
                                src[:, :, half - 1:half].broadcast_to([P, blocks, 2 * half]),
                                ALU.subtract).then_inc(dl_ready, 1)

            def collect(level):
                for tt in range(NT if level < 8 else 1):
                    dve.wait_ge(lev_ready, t.take(lev_ready))
                    src = banks[D0 + tt].rearrange("p a (b c) -> p (a b) c", c=P)
                    if level == 8:
                        v.tensor_copy(gs0[:, :, P:S], src).then_inc(lev_used, 1)
                    else:
                        mask = c_("levels", P * level, P).bitcast(I32).unsqueeze(1).broadcast_to([P, 4, P])
                        v.copy_predicated((gs0[:, :, 0:P], gs1)[tt], mask, src).then_inc(lev_used, 1)
                    dve.wait_ge(lev_used, t.take(lev_used))

            for n in range(GLA, GLA_OUT):
                split_lo(n + 2)
                if n > GLA:
                    freed(n - 1)
                if n == GLA + 1:
                    own(v.memset(gs0, 0.0))
                    chain(v.memset(gs1, 0.0))
                if n == GLA + 2:
                    dve.wait_ge(gz_ready, 1)
                    for c in range(4):
                        ins = v.tensor_scalar(gz[:, c, :], banks[(M0, D0)[c // 2]][:, c % 2, :], p_("gate_bias", c), None,
                                              ALU.add)
                        if c < 3:
                            own(ins)
                    ins.then_inc(gz_read, 1)
                    dve.wait_ge(ln_ready, 1)
                    chain(v.scalar_tensor_tensor(gz, gz, 0.0, gzl, ALU.min, ALU.subtract))
                    for c in range(4):
                        ins = v.tensor_tensor_scan(gg[:, c, :], ones4, gz[:, c, :], 0.0, ALU.mult, ALU.add)
                        if c < 3:
                            own(ins)
                    ins.then_inc(gg_ready, 1)
                    dve.wait_ge(gg_ready, 1)
                if GLA + 4 <= n <= GLA + 11:
                    collect(n - GLA - 4)
                if GLA + 3 <= n <= GLA + 10:
                    distance(n - GLA - 2)
            collect(8)
            freed(GLA_OUT - 1)
            for h in range(4):
                if h % 2 == 0:
                    dve.wait_ge(ort_ready, h // 2 + 1)
                for c in range(2):
                    done = own(v.scalar_tensor_tensor(on[h][:, c, :], banks[D0 + h][:, c, :], p_("o_norm", c),
                                                      ort[:, h, :], ALU.mult, ALU.mult))
                dve.wait_ge(dve_done, done)
                v.tensor_tensor(on[h], on[h], gog[:, 2 * h:2 * h + 2, :], ALU.mult).then_inc(on_ready, 1)
                if h:
                    out_lo(a_lo[:, 2 * h - 2:2 * h, :], on[h - 1], a_hi[:, 2 * h - 2:2 * h, :])
            out_lo(a_lo[:, 6:8, :], on[3], a_hi[:, 6:8, :])
            for n in range(GLA_OUT, FFN1):
                split_lo(n + 2)
                if n > GLA_OUT:
                    residual(n - 1, n - 1 - GLA_OUT)
            residual(FFN1 - 1, 3)
            norm(x, lambda k: p_("ffn_norm1", k), a_hi, a_lo)
            ffn(FFN1, "conv1", True, add_plain)

            def modulation_vectors():
                dve.wait_ge(mod_done, MOD_TILES)
                chain(v.tensor_tensor(mod, banks[M1].rearrange("p a b -> p (a b)")[:, 0:2 * MOD_OUT]
                                      .rearrange("p (a b) -> p a b", b=2),
                                      p_("b_mod", 0, MOD_OUT).unsqueeze(2).broadcast_to([P, MOD_OUT, 2]), ALU.add))
                for which in range(2):
                    done = own(v.scalar_tensor_tensor(scale1[:, which, :], mod[:, 8:16, which], 1.0, p_("norm1", 0, 8),
                                                      ALU.add, ALU.mult))
                dve.wait_ge(dve_done, done)

            def context_norm(c):
                if c == 0:
                    modulation_vectors()
                norm(cx, lambda k: scale1[:, 1, k:k + 1], c_hi, c_lo, lambda k: mod[:, k, 1:2],
                     range(2 * c, 2 * c + 2))

            ple(PLE1, 1, context_norm)

            norm(x, lambda k: scale1[:, 0, k:k + 1], a_hi, a_lo, lambda k: mod[:, k, 0:1])
            own(v.memset(mh[:, :, 0:pad], 0.0))
            own(v.memset(mh[:, :, pad + S:], 0.0))
            groups = [mk[:, :, S:2 * S], mk[:, :, 0:S]] + [mq[:, 2 * j:2 * j + 2, :] for j in range(4)]
            gains = [p_("k_g"), p_("k_g")] + 4 * [p_("q_g")]

            divided = set()

            def mix_divide(u):
                if 0 <= u < 16 and u not in divided:
                    divided.add(u)
                    sm = small[:, u % 2]
                    dve.wait_ge(att_e, t.take(att_e))
                    chain(v.reciprocal(sm[:, 3, 0:1], sm[:, 2, 0:1]))
                    e = e_sb[u % 2]
                    v.tensor_scalar(e, e, sm[:, 3, 0:1], None, ALU.mult).then_inc(att_p, 1)

            def mix_unit(i):
                if i >= 4 and i % 2 == 0:
                    h = (i - 4) // 2
                    out_lo(o_lo[:, h, :], banks[M0 + h % 2][:, 0, :], o_hi[:, h, :])
                mix_divide(i - 1)
                if i < 16:
                    sm = small[:, i % 2]
                    dve.wait_ge(att_s, t.take(att_s))
                    chain(v.tensor_reduce(sm[:, 0, 0:1], banks[D0 + i % 2].rearrange("p a b -> p (a b)"), AX_X, ALU.max))
                    v.tensor_scalar(sm[:, 1, 0:1], sm[:, 0, 0:1], -MIX_SCALE, None, ALU.mult).then_inc(att_m, 1)

            conv_done = [0] * DVE_CONV

            def conv_taps(a, b):
                for tap in range(a, b):
                    for c in range(DVE_CONV):
                        if tap > 1:
                            dve.wait_ge(dve_done, conv_done[c])
                        ins = v.scalar_tensor_tensor(acc[:, c, :], mh[:, c, tap:tap + S], p_("dw", 31 * c + tap),
                                                     acc[:, c, :], ALU.mult, ALU.add)
                        if (tap, c) == (30, DVE_CONV - 1):
                            ins.then_inc(conv_ready, 1)
                        else:
                            conv_done[c] = own(ins)

            def mix_post(n):
                freed(n)
                j, b = n - MIX, n % 2
                if j in (4, 5):
                    pair = slice(2 * j - 8, 2 * j - 6)
                    dve.wait_ge(bank_free[b], t.now(bank_free[b]))
                    v.scalar_tensor_tensor(mh[:, pair, pad:pad + S], (gate_c, up_c)[j % 2], 1.0, ma[:, pair, :],
                                           ALU.add, ALU.mult).then_inc(mh_ready, 1)
                if 18 <= j < 22:
                    results(n)
                    pair = mg[:, 2 * j - 36:2 * j - 34, :]
                    v.scalar_tensor_tensor(pair, pair, 1.0, banks[b], ALU.add, ALU.mult).then_inc(bank_free[b], 1)
                if j >= 22:
                    results(n)
                    pairs = [mg[:, KC + 2 * c:KC + 2 * c + 2, :] for c in (2 * j - 44, 2 * j - 43)]
                    for b, pair in zip((G, U), pairs):
                        v.scalar_tensor_tensor(pair, pair, 1.0, banks[co_banks(n)[b]], ALU.add,
                                               ALU.mult).then_inc(bank_free[b], 1)
                    for b, pair in zip((G, U), pairs):
                        c = 2 * (j - 22) + b
                        dve.wait_ge(bank_free[b], t.now(bank_free[b]))
                        v.tensor_tensor(pair, pair, mg[:, 2 * c:2 * c + 2, :], ALU.add).then_inc(mixed, 1)

            def mix_lo(pair):
                for j in (pair, pair + 1):
                    k = slice(2 * j, 2 * j + 2)
                    dve.wait_ge(y_hi_ready, t.take(y_hi_ready))
                    v.scalar_tensor_tensor(a_lo[:, k, :], mg[:, KC + 2 * j:KC + 2 * j + 2, :], 0.5,
                                           a_hi[:, k, :].bitcast(F32), ALU.mult, ALU.subtract).then_inc(y_ready, 1)

            for n in range(MIX, MIX_OUT):
                j = n - MIX
                if j > 18:
                    mix_post(n - 1)
                if j == 23:
                    mix_lo(0)
                split_lo(n + 2)
                if 0 < j <= 18:
                    mix_post(n - 1)
                if j - 1 in HEAD_STEPS and HEAD_STEPS[j - 1] != 1:
                    rotate(groups[HEAD_STEPS[j - 1]], c_("cos"), c_("sin"))
                if j in HEAD_STEPS:
                    head_norm(groups[HEAD_STEPS[j]], gains[HEAD_STEPS[j]])
                for i in MIX_UNITS.get(n, ()):
                    mix_unit(i)
                if n == MIX_AO:
                    mix_unit(18)
                if j == 6:
                    dve.wait_ge(conv_base, t.take(conv_base, DVE_CONV))
                if 6 <= j < 18:
                    conv_taps(1 + 5 * (j - 6) // 2, 1 + 5 * (j - 5) // 2)
                if n in MIX_UNITS:
                    mix_divide(MIX_UNITS[n][-1])
                if n == MIX_AO:
                    dve.wait_ge(mu_ready, 1)
                    v.tensor_tensor(acc, acc, hrt[:, 0:1, :].broadcast_to([P, 4, S]), ALU.subtract).then_inc(cen_ready, 1)
                if n == MIX_AO + 1:
                    dve.wait_ge(lrt_ready, 1)
                    v.tensor_tensor(acc, acc, hrt[:, 1:2, :].broadcast_to([P, 4, S]), ALU.mult).then_inc(ln_n_ready, 1)
                    dve.wait_ge(lhi_ready, 1)
                    v.tensor_tensor(l_lo, lsq, l_hi.bitcast(F32), ALU.subtract).then_inc(l_ready, 1)
            mix_post(MIX_OUT - 1)
            mix_lo(2)

            def gated_residual(n, j):
                results(n)
                freed(n)
                for c in range(2):
                    k = 2 * j + c
                    ins = v.scalar_tensor_tensor(x[:, k, :], banks[n % 2][:, c, :], mod[:, 16 + k, 0:1], x[:, k, :],
                                                 ALU.mult, ALU.add)
                    if c:
                        ins.then_inc(bank_free[n % 2], 1)
                    else:
                        own(ins)

            for n in range(MIX_OUT, FFN2):
                split_lo(n + 2)
                if n > MIX_OUT:
                    gated_residual(n - 1, n - 1 - MIX_OUT)
            chain(v.scalar_tensor_tensor(scale1[:, 2, :], mod[:, 32:40, 0], 1.0, p_("norm2", 0, 8), ALU.add, ALU.mult))
            gated_residual(FFN2 - 1, 3)
            norm(x, lambda k: scale1[:, 2, k:k + 1], a_hi, a_lo, lambda k: mod[:, 24 + k, 0:1])
            ffn(FFN2, "conv2", False, add_gated)
            norm(x, lambda k: p_("final", k))

        @block.gpsimd
        def _(pool):
            def modulation(m, both, turn=None):
                at = lambda k: k if turn is None else turn + k
                if not (turn is None and m == 0):
                    pool.wait_ge(mod_added, at(m))
                pool.wait_ge(mod_landed, at(m + 1) * 16)
                for which in range(1 + both):
                    scale = silu_c[:, :, which:which + 1].broadcast_to([P, KC, 256])
                    ins = nc.gpsimd.tensor_tensor(mod_mul[which], mod_raw, scale, ALU.mult)
                    ins.then_inc(mod_taken if which == both else pool_half, 1)
                pool.wait_ge(mod_taken, at(m + 1))
                for k in (4, 2, 1):
                    for which in range(1 + both):
                        a = mod_mul[which]
                        dst = a[:, 0:k, :] if k > 1 else mod_sum[:, which:which + 1, :]
                        if k == 1 and which == 0 and not (turn is None and m == 0):
                            pool.wait_ge(mod_done, at(m))
                        ins = nc.gpsimd.tensor_tensor(dst, a[:, 0:k, :], a[:, k:2 * k, :], ALU.add)
                        if which == both:
                            ins.then_inc((mod_four, mod_two, mod_added)[(4, 2, 1).index(k)], 1)
                    if k > 1:
                        pool.wait_ge((mod_four, mod_two)[(4, 2).index(k)], at(m + 1))

            pool.wait_ge(silu_ready, 1)
            modulation(0, 1)
            with pool.Fori(0, MOD_BOTH - 1, 1) as turn:
                modulation(1, 1, turn)
            with pool.Fori(0, MOD_FFN1 - 1 - MOD_BOTH, 1) as turn:
                modulation(MOD_BOTH, 0, turn)
            for level in range(1, 9):
                pool.wait_ge(ee_ready, level)
                if level >= 3:
                    pool.wait_ge(lev_ready, 2 * (level - 1))
                k = level % 2
                nc.gpsimd.tensor_tensor(gqp[k], gq, dl[k], ALU.mult)
                if level == 1:
                    b = (GLA + 3) % 2
                    pool.wait_ge(bank_free[b], sum(b in banks_of(n) for n in range(GLA + 4)))
                nc.gpsimd.tensor_tensor(gkp[k], gk, dl[k], ALU.mult).then_inc(qk_ready, 1)
            with pool.Fori(0, MOD_TILES - MOD_FFN1 + 1, 1) as turn:
                modulation(MOD_FFN1 - 1, 0, turn)
            pool.wait_ge(mh_ready, 2)
            done = 0
            for c in range(DVE_CONV, 4):
                for tap in range(31):
                    tmp = mtmp[tap % 2]
                    dst = tmp if tap else acc[:, c, :]
                    nc.gpsimd.tensor_scalar(dst, mh[:, c, tap:tap + S], p_("dw", 31 * c + tap),
                                            p_("dw_b", c) if tap == 0 else None, ALU.mult,
                                            *([ALU.add] if tap == 0 else [])).then_inc(pool_done, 1)
                    done += 1
                    if tap:
                        pool.wait_ge(pool_done, done)
                        nc.gpsimd.tensor_tensor(acc[:, c, :], acc[:, c, :], tmp, ALU.add).then_inc(pool_done, 1)
                        done += 1
            pool.wait_ge(pool_done, done)
            nc.gpsimd.tensor_copy(mtmp[0][:, 0:1], acc[:, 3, 0:1]).then_inc(pool_conv, 1)

        @block.tensor
        def _(pe):
            t = Tally()
            reader = {}
            token = {}
            mm = nc.tensor.matmul

            def use(bank, sem_, k=1):
                if bank in reader:
                    pe.wait_ge(*reader[bank])
                reader[bank] = (sem_, t.take(sem_, k))

            def open_tile(n, turn=None, fresh=False, behind=0):
                pe.wait_ge(lo_ready, n + 1 if turn is None else turn * SLOTS + (n + 1))
                token[n] = []
                for b in banks_of(n):
                    if not fresh and t.count.get(bank_free[b].name):
                        pe.wait_ge(bank_free[b], t.now(bank_free[b], behind))
                    token[n].append((bank_free[b], t.take(bank_free[b])))

            def three(out, hi, lo, r_hi, r_lo, start, stop):
                mm(out, hi, r_hi, start=start, stop=False, skip_group_check=True)
                mm(out, hi, r_lo, start=False, stop=False, skip_group_check=True)
                return mm(out, lo, r_hi, start=False, stop=stop, skip_group_check=True)

            def columns(n, src_hi=None, src_lo=None, ready=None, order=range(KC), bank=None, out=2, begin=True,
                        end=True, middle=None):
                src_hi, src_lo = (a_hi, a_lo) if src_hi is None else (src_hi, src_lo)
                b = banks[banks_of(n)[0] if bank is None else bank]
                s = n % SLOTS
                last = len(order) - 1
                steps = [(i, k, j) for i, k in enumerate(order) for j in range(out)]
                if not ready:
                    steps.sort(key=lambda step: step[2])
                for i, k, j in steps:
                    if ready and j == 0:
                        ready(i)
                    if middle and (i, j) == (0, 1):
                        middle()
                    col = slice(256 * k + P * j, 256 * k + P * j + P)
                    ins = three(b[:, j, :], w_hi[s][:, col], w_lo[s][:, col], src_hi[:, k, :], src_lo[:, k, :],
                                begin and i == 0 and (j == 0 or not ready), end and i == last)
                return ins

            def columns_part(n, j, order, begin):
                s = n % SLOTS
                for i, k in enumerate(order):
                    col = slice(256 * k + P * j, 256 * k + P * j + P)
                    ins = three(banks[n % 2][:, j, :], w_hi[s][:, col], w_lo[s][:, col], a_hi[:, k, :], a_lo[:, k, :],
                                begin and i == 0 and j == 0, not begin and i == len(order) - 1)
                return ins

            def tokens_major(n, bank, src_hi, src_lo, col, width, base=0):
                s = n % SLOTS
                flat = banks[bank].rearrange("p a b -> p (a b)")
                for tt in range(NT):
                    for k in range(KC):
                        at = slice(256 * k + col, 256 * k + col + width)
                        out = flat[:, base + tt * width:base + (tt + 1) * width]
                        cols = slice(P * tt, P * tt + P)
                        mm(out, src_hi[:, k, cols], w_hi[s][:, at], start=(k == 0), stop=False, skip_group_check=True)
                        mm(out, src_hi[:, k, cols], w_lo[s][:, at], start=False, stop=False, skip_group_check=True)
                        ins = mm(out, src_lo[:, k, cols], w_hi[s][:, at], start=False, stop=(k == KC - 1),
                                 skip_group_check=True)
                return ins

            def rows(n, first, last, turn=None):
                s = n % SLOTS
                pe.wait_ge(h_ready, t.take(h_ready))
                r_hi, r_lo = (a_hi, a_lo) if last and not first else (h_hi, h_lo)
                order = [(kk, c) for kk in range(2) for c in range(KC)]
                if last:
                    order.sort(key=lambda step: step[1] // 2)
                for kk, c in order:
                    col = slice(D * kk + P * c, D * kk + P * c + P)
                    ins = three(banks[D0 + c // 2][:, c % 2, :], w_hi[s][:, col], w_lo[s][:, col],
                                r_hi[:, kk, :], r_lo[:, kk, :], first and kk == 0 and c % 2 == 0,
                                last and kk == 1)
                    if last and not first and kk == 1 and c % 2 and c < KC - 1:
                        ins.then_inc(d_ready, 1)
                if last and not first:
                    ins.then_inc(d_ready, 1)
                    ins = mm(banks[M0][:, 0, 0:2], c_("ones"), c_("ones", 0, 2), start=True, stop=True)
                ins.then_inc(tile_used, 1)

            def norm_ready(i):
                pe.wait_ge(n_ready, t.take(n_ready))

            def norm():
                use(M0, rt_ready)
                for k in range(KC):
                    if k % 2 == 0:
                        pe.wait_ge(sq_ready, t.take(sq_ready))
                    ins = mm(banks[M0][:, 0, :], c_("ones"), nrm[:, k, :], start=(k == 0), stop=(k == KC - 1))
                ins.then_inc(ss_ready, 1)

            def modulation(m, turn=None):
                pe.wait_ge(mod_added, m + 1 if turn is None else turn + (m + 1))
                flat = banks[M1].rearrange("p a b -> p (a b)")
                for j in range(2):
                    for which in range(2):
                        col = 4 * m + 2 * j + which
                        out = flat[:, col:col + 1] if turn is None else flat[:, bass.ds(turn * 4 + col, 1)]
                        ins = mm(out, mod_sum[:, which, P * j:P * j + P], c_("one"), start=True, stop=True)
                ins.then_inc(mod_done, 1)

            def ffn(first, m=None):
                def pair_steps(n, begin, turn=None):
                    open_tile(n, turn)
                    columns(n).then_inc(tile_used, 1)
                    open_tile(n + 1, turn)
                    columns(n + 1).then_inc(tile_used, 1)
                    open_tile(n + 2, turn)
                    rows(n + 2, begin, False)

                open_tile(first)
                columns(first, ready=norm_ready).then_inc(tile_used, 1)
                open_tile(first + 1)
                columns(first + 1).then_inc(tile_used, 1)
                for j in range(4):
                    use(D0 + j, res_ready)
                pair_steps(first + 2, True)
                turns = FFN_TURNS - 1
                with pe.Fori(0, turns, 1) as turn:
                    t.loop(turn, {bank_free[G]: 1, bank_free[U]: 1, h_ready: 1})
                    pair_steps(first + 5, False, turn)
                    if m is not None:
                        modulation(m, turn)
                t.end(turns)
                for pair in range(2 + turns, FP):
                    pair_steps(first + 3 * pair - 1, False)
                if m is not None:
                    modulation(m + turns)
                open_tile(first + FFN_TILES - 1)
                rows(first + FFN_TILES - 1, False, True)

            def ple(first, m, after=None):
                norm()
                open_tile(first)
                for j in range(4):
                    use(D0 + j, res_ready)
                rows(first, True, True)
                modulation(m)
                for c in range(4):
                    open_tile(first + 1 + c)
                    columns(first + 1 + c, ready=None if c else norm_ready).then_inc(tile_used, 1)
                    if c == 0 and after:
                        after()

            def head_sum(width, which):
                pe.wait_ge(hsq_ready, t.take(hsq_ready))
                group = t.now(hsq_ready) - 1
                group -= 3 if group >= 3 else 0
                use(M0, hrt_ready)
                mm(banks[M0][:, 0:width, :], c_(which), hsq[group % 2][:, 0:width, :], start=True,
                   stop=True).then_inc(hss_ready, 1)

            def swap(raw, which):
                pe.wait_ge(hn_ready, t.take(hn_ready))
                use(D0, hrot_used)
                mm(banks[D0][:, 0:raw.shape[1], :], c_(which), raw, start=True, stop=True).then_inc(hrot_ready, 1)

            pe.wait_ge(con_in, 16)
            norm()
            hy_raw = [hy_q[:, 0:2, :], hy_q[:, 2:4, :], hy_k.unsqueeze(1)]

            def hy_unit(i):
                if 1 <= i < 9:
                    u = i - 1
                    blocks = u // 4 + 1
                    pe.wait_ge(att_p, t.take(att_p))
                    use(D0 + 2 + u % 2, att_pt)
                    out = banks[D0 + 2 + u % 2].rearrange("p a (b c) -> p (a b) c", c=P)
                    for g in range(2):
                        for b in range(blocks):
                            ins = nc.tensor.transpose(out[:, g * blocks + b, :], e_sb[u % 2][:, g, P * b:P * b + P],
                                                      c_("eye"))
                    ins.then_inc(att_t, 1)
                if i < 8:
                    if i == 0:
                        pe.wait_ge(rope_ready, t.take(rope_ready, 3))
                    tt, c = i // 4, i % 4
                    w = P * (tt + 1)
                    use(D0 + i % 2, att_masked)
                    for g in range(2):
                        rows_ = slice(64 * g, 64 * g + 64)
                        ins = mm(banks[D0 + i % 2][:, g, 0:w], hy_q[rows_, c, P * tt:P * tt + P], hy_k[rows_, 0:w],
                                 start=True, stop=True)
                        if g == 0:
                            ins.then_inc(att_half, 1)
                            pe.wait_ge(att_half, i + 1)
                    ins.then_inc(att_s, 1)
                if 2 <= i < 10:
                    u = i - 2
                    tt, c, blocks = u // 4, u % 4, u // 4 + 1
                    if u == 0:
                        pe.wait_ge(*token[HY_KV][0])
                    if c == 0:
                        use(M0, hy_o_ready)
                    pe.wait_ge(att_pt, u + 1)
                    out = banks[M0].rearrange("p a (b c) -> p (a b) c", c=P)
                    for g in range(2):
                        for b in range(blocks):
                            ins = mm(out[64 * g:64 * g + 64, c, :], hy_v[:, b, 64 * g:64 * g + 64],
                                     pt_sb[u % 2][:, g * blocks + b, :], start=(b == 0), stop=(b == blocks - 1))
                    ins.then_inc(att_o, 1)

            for n in range(HY_OUT):
                open_tile(n)
                if n == HY_KV:
                    columns(n, out=1)
                    ins = tokens_major(n, banks_of(n)[0], a_hi, a_lo, P, P, base=S)
                else:
                    units = HY_UNITS.get(n, ())
                    ins = columns(n, ready=norm_ready if n == 0 else None,
                                  middle=(lambda: hy_unit(units[0])) if units else None)
                ins.then_inc(tile_used, 1)
                if 2 <= n <= 4:
                    swap(hy_raw[n - 2], "rope_half")
                if 1 <= n <= 3:
                    head_sum(2 if n < 3 else 1, "ones_head")
                for i in HY_UNITS.get(n, ())[1:]:
                    hy_unit(i)
                if n in MOD_HY:
                    modulation(MOD_HY[n])

            def y_wait(upto):
                def ready(i):
                    if upto[i]:
                        pe.wait_ge(y_ready, t.take(y_ready, upto[i]))
                return ready

            conv_k, att_k = [4, 5, 6, 7], [0, 1, 2, 3]
            open_tile(HY_OUT)
            columns(HY_OUT, ready=y_wait([1, 0, 1, 0]), order=conv_k, end=False)
            hy_unit(8)
            open_tile(HY_OUT + 1)
            for j in range(2):
                columns_part(HY_OUT + 1, j, conv_k, True)
                hy_unit(9 + j)
            columns(HY_OUT, ready=y_wait([2, 0, 0, 0]), order=att_k, begin=False).then_inc(tile_used, 1)
            for j in range(2):
                ins = columns_part(HY_OUT + 1, j, att_k, False)
            ins.then_inc(tile_used, 1)
            modulation(MOD_HY[HY_OUT])
            for n in range(HY_OUT + 2, FFN0):
                open_tile(n)
                columns(n).then_inc(tile_used, 1)
            modulation(MOD_HY[HY_OUT + 3])
            norm()
            ffn(FFN0, MOD_FFN0)
            ple(PLE0, MOD_FFN0 + FFN_TURNS)

            norm()

            def level_scores(level):
                q, k = (gq, gk) if level == 0 else (gqp[level % 2], gkp[level % 2])
                if level:
                    pe.wait_ge(qk_ready, level)
                else:
                    pe.wait_ge(*token[GLA + 3][0])
                    pe.wait_ge(*token[GLA + 2][0])
                for tt in range(NT if level < 8 else 1):
                    use(D0 + tt, lev_used)
                    keys = slice(P * tt, P * tt + P)
                    queries = keys if level < 8 else slice(P, S)
                    out = banks[D0 + tt].rearrange("p a (b c) -> p (a b) c", c=P)
                    for h in range(4):
                        ins = mm(out[:, h, :], k[:, h, keys], q[:, h, queries], start=True, stop=True)
                    ins.then_inc(lev_ready, 1)

            for n in range(GLA, GLA_OUT):
                open_tile(n)
                if GLA + 4 <= n < GLA + 8:
                    ins = tokens_major(n, banks_of(n)[0], a_hi, a_lo, 0, 256)
                else:
                    ins = columns(n, ready=norm_ready if n == GLA else None)
                ins.then_inc(tile_used, 1)
                if n == GLA:
                    use(M0, glr_copied)
                    for k in range(KC):
                        ins = mm(banks[M0][0:16, 0, :], p_("glr_w", 16 * k, 16), nrm[:, k, :], start=(k == 0),
                                 stop=(k == KC - 1))
                    ins.then_inc(glr_ready, 1)
                if n == GLA + 1:
                    pe.wait_ge(glr_copied, 1)
                    pe.wait_ge(late_in, 32)
                    use(D0, gz_read)
                    for c in range(4):
                        ins = mm(banks[(M0, D0)[c // 2]][:, c % 2, :], up_w[:, P * c:P * c + P], glr, start=True, stop=True)
                    ins.then_inc(gz_ready, 1)
                    reader[M0] = (gz_read, 1)
                if n == GLA + 4:
                    level_scores(0)
                if n >= GLA + 4:
                    level_scores(n - GLA - 3)
            pe.wait_ge(*token[GLA + 7][0])
            pe.wait_ge(*token[GLA + 6][0])
            pe.wait_ge(lev_used, t.now(lev_used))
            for h in range(4):
                pe.wait_ge(*reader[D0 + h])
                reader[D0 + h] = (y_ready, t.now(y_ready) + h + 1)
                for c in range(2):
                    cols = slice(256 * h + P * c, 256 * h + P * c + P)
                    mm(banks[D0 + h][:, c, :], gv[:, 0, cols], gs0[:, h, :], start=True, stop=False,
                       skip_group_check=True)
                    ins = mm(banks[D0 + h][:, c, P:S], gv[:, 1, cols], gs1[:, h, :], start=False, stop=True,
                             skip_group_check=True)
                ins.then_inc(go_ready, 1)
            for h in range(4):
                pe.wait_ge(osq_ready, h + 1)
                if h % 2 == 0:
                    use(M0, ort_ready)
                for c in range(2):
                    ins = mm(banks[M0][:, h % 2, :], c_("ones"), osq[h][:, c, :], start=(c == 0), stop=(c == 1))
                if h % 2:
                    ins.then_inc(oss_ready, 1)
            open_tile(GLA_OUT)
            columns(GLA_OUT, ready=y_wait([1, 0, 1, 0, 1, 0, 1, 0])).then_inc(tile_used, 1)
            for n in range(GLA_OUT + 1, FFN1):
                open_tile(n)
                columns(n).then_inc(tile_used, 1)
            modulation(MOD_FFN1 - 1)
            norm()
            ffn(FFN1, MOD_FFN1)
            ple(PLE1, MOD_FFN1 + FFN_TURNS, norm)

            norm()
            t.take(att_e, 8)
            groups = [mk[:, :, S:2 * S], mk[:, :, 0:S]] + [mq[:, 2 * j:2 * j + 2, :] for j in range(4)]

            def mix_unit(i):
                if 1 <= i < 17:
                    u = i - 1
                    pe.wait_ge(att_p, t.take(att_p))
                    use(D0 + 2 + u % 2, att_pt)
                    out = banks[D0 + 2 + u % 2].rearrange("p a (b c) -> p (a b) c", c=P)
                    e = e_sb[u % 2].rearrange("p a (b c) -> p (a b) c", c=P)
                    for b in range(4):
                        ins = nc.tensor.transpose(out[:, b, :], e[:, b, :], c_("eye"))
                    ins.then_inc(att_t, 1)
                if i < 16:
                    if i % 4 == 0:
                        pe.wait_ge(rope_ready, t.take(rope_ready, 2 if i == 0 else 1))
                    if i == 0:
                        pe.wait_ge(hn_ready, 5)
                    h, tt = i // 2, i % 2
                    use(D0 + i % 2, att_e)
                    mm(banks[D0 + i % 2].rearrange("p a b -> p (a b)"), mq[:, h, P * tt:P * tt + P], mk[:, h // 4, :],
                       start=True, stop=True).then_inc(att_s, 1)
                if 2 <= i < 18:
                    u = i - 2
                    h, tt = u // 2, u % 2
                    if u == 0:
                        for tok in token[MIX + 1]:
                            pe.wait_ge(*tok)
                    if tt == 0:
                        use(M0 + h % 2, y_ready)
                    pe.wait_ge(att_pt, 8 + u + 1)
                    for b in range(4):
                        ins = mm(banks[M0 + h % 2][:, 0, P * tt:P * tt + P], mv[:, b, P * (h // 4):P * (h // 4) + P],
                                 pt_sb[u % 2][:, b, :], start=(b == 0), stop=(b == 3))
                    ins.then_inc(att_o, 1)

            def head_chunk(i):
                pe.wait_ge(y_ready, t.now(y_ready, KC - 1 - i))

            for n in range(MIX, MIX_OUT):
                j = n - MIX
                open_tile(n, fresh=n == MIX_CO + 1)
                if j == 0:
                    pe.wait_ge(n_ready, t.take(n_ready, KC))
                    pe.wait_ge(*reader[D0 + 2])
                    reader[D0 + 2] = token[n][0]
                    columns(n, c_hi, c_lo, bank=D0 + 2)
                    ins = columns(n, ready=norm_ready)
                elif j == 1:
                    pe.wait_ge(*reader[D0 + 3])
                    reader[D0 + 3] = token[n][0]
                    tokens_major(n, D0 + 3, c_hi, c_lo, 0, 256)
                    ins = tokens_major(n, banks_of(n)[0], a_hi, a_lo, 0, 256)
                elif 18 <= j < 22:
                    ins = columns(n, o_hi, o_lo, ready=head_chunk if j == 18 else None)
                elif j >= 22:
                    if j == 22:
                        pe.wait_ge(l_ready, 1)
                    else:
                        for b in (1, 2):
                            pe.wait_ge(*reader[D0 + b])
                            reader[D0 + b] = token[n][b - 1]
                    s = n % SLOTS
                    for k in range(4):
                        for c in range(4):
                            col = slice(512 * k + P * c, 512 * k + P * c + P)
                            ins = three(banks[co_banks(n)[c // 2]][:, c % 2, :], w_hi[s][:, col], w_lo[s][:, col],
                                        l_hi[:, k, :], l_lo[:, k, :], k == 0 and c % 2 == 0, k == 3)
                else:
                    units = MIX_UNITS.get(n, ())
                    ins = columns(n, middle=(lambda: mix_unit(units[0])) if units else None)
                ins.then_inc(tile_used, 1)
                if j in HEAD_STEPS and HEAD_STEPS[j] != 1:
                    swap(groups[HEAD_STEPS[j]], "rope_pair")
                if j == 3:
                    t.take(hn_ready)
                if j + 1 in HEAD_STEPS:
                    head_sum(2, "ones")
                for i in MIX_UNITS.get(n, ())[1:]:
                    mix_unit(i)
                if n == MIX_AO - 1:
                    pe.wait_ge(conv_ready, 1)
                    pe.wait_ge(pool_conv, 1)
                    use(M0, mu_ready)
                    for c in range(4):
                        ins = mm(banks[M0][:, 0, :], c_("ones"), acc[:, c, :], start=(c == 0), stop=(c == 3))
                    ins.then_inc(lm_ready, 1)
                if n == MIX_AO:
                    pe.wait_ge(lsq_ready, 1)
                    use(D0, lrt_ready)
                    for c in range(4):
                        ins = mm(banks[D0][:, 0, :], c_("ones"), lsq[:, c, :], start=(c == 0), stop=(c == 3))
                    ins.then_inc(lv_ready, 1)
            open_tile(MIX_OUT, behind=1)
            columns(MIX_OUT, ready=y_wait([1, 0, 1, 0, 1, 0, 1, 0])).then_inc(tile_used, 1)
            for n in range(MIX_OUT + 1, FFN2):
                open_tile(n, behind=int(n == MIX_OUT + 1))
                columns(n).then_inc(tile_used, 1)
            norm()
            ffn(FFN2)
            norm()


def columns_tile(w, at, k=KC, width=256):
    return w[:, at:at + width].reshape(k, P, width).transpose(1, 0, 2).reshape(P, k * width)


def rows_tile(w, at):
    return w[at:at + 256].reshape(2, P, D).transpose(1, 0, 2).reshape(P, 2 * D)


def feed_forward_tiles(up, down):
    tiles = []
    for i in range(FP):
        tiles += [columns_tile(up, 256 * i), columns_tile(up, FF + 256 * i)]
        if i:
            tiles.append(rows_tile(down, 256 * (i - 1)))
    return tiles + [rows_tile(down, 256 * (FP - 1))]


def by_partition(v):
    v = v.reshape(v.shape[:-1] + (-1, P))
    return np.moveaxis(v, (-1, -2), (0, 1))


def feature_major(a):
    return np.ascontiguousarray(by_partition(a))


def constants():
    one = np.eye(P, dtype=np.float32)
    out = {"ones": np.ones((P, P)), "eye": one, "eps": np.full((P, 1), EPS), "one": np.ones((P, 1))}
    head = np.arange(P) // 64
    out["ones_head"] = head[:, None] == head[None, :]
    half, pair = np.zeros((P, P)), np.zeros((P, P))
    for m in range(P):
        lower = m % 64 < 32
        half[m + 32 if lower else m - 32, m] = -1 if lower else 1
        pair[m ^ 1, m] = -1 if m % 2 == 0 else 1
    out["rope_half"], out["rope_pair"] = half, pair
    s, q = np.arange(P)[:, None], np.arange(P)[None, :]
    levels = [s == q]
    for level in range(1, 8):
        h = 1 << (level - 1)
        levels.append((s // (2 * h) == q // (2 * h)) & (s % (2 * h) < h) & (q % (2 * h) >= h))
    out["levels"] = np.concatenate(levels, 1)
    out["window"] = np.concatenate([np.where(q > s, 0.0, NEG), np.where(q <= s, 0.0, NEG)], 1)
    freq = np.float32(10000.0) ** (-np.arange(0, 64, 2, dtype=np.float32) / np.float32(64))
    out["inv_freq"] = freq[np.arange(P) % 32][:, None]
    tok = np.arange(S)
    ang = np.concatenate([(tok // 64).astype(np.float32)[:, None] * freq,
                          (tok % 64).astype(np.float32)[:, None] * freq], 1)
    ang = np.repeat(ang, 2, axis=1).T
    out["cos"], out["sin"] = np.cos(ang), np.sin(ang)
    return np.ascontiguousarray(np.concatenate([out[name].astype(np.float32) for name in CONSTS], 1))


def kernel(**inputs):
    import concourse.bacc as _bacc
    from concourse import mybir as _mybir
    from concourse.bass_utils import run_bass_kernel_spmd as _run

    a = {name: np.asarray(value) for name, value in inputs.items()}

    w = a["hy_w_in"][0]
    heads = np.concatenate([np.arange(64 * h, 64 * h + 64) for c in range(4) for h in (c, 4 + c)])
    w = np.concatenate([w[:, heads], w[:, 512:768], w[:, 1280:1792], w[:, 1792:2304], w[:, 768:1280]], 1)
    w_out = np.concatenate([a["hy_w_out"][0][heads], a["hy_w_out"][0][512:]], 0)
    tiles = [columns_tile(w, 256 * i) for i in range(9)]
    tiles += [columns_tile(w_out, 256 * i) for i in range(4)]

    def per_layer(i):
        out = feed_forward_tiles(a["ffn_w_up"][i], a["ffn_w_down"][i])
        out.append(rows_tile(a["ple_w_proj"][i], 0))
        return out + [columns_tile(a["ple_w_gate"][i], 256 * j) for j in range(4)]

    tiles += per_layer(0)
    w = a["gla_w_in"][0]
    tiles += [columns_tile(w, 256 * i) for i in range(8)]
    tiles += [columns_tile(w, 2064 + 256 * i) for i in range(4)]
    tiles += [columns_tile(a["gla_w_out"][0], 256 * i) for i in range(4)]
    tiles += per_layer(1)
    w = a["w_in_2"][0]
    tiles += [columns_tile(w, at) for at in (1024, 1280)]
    tiles += [columns_tile(w, at + 256 * i) for at, many in ((1536, 4), (0, 4), (2560, 8)) for i in range(many)]
    tiles += [columns_tile(a["w_attn_out_2"][0], 256 * i) for i in range(4)]
    tiles += [columns_tile(a["w_conv_out_2"][0], 512 * i, 4, 512) for i in range(2)]
    tiles += [columns_tile(a["w_out_2"][0], 256 * i) for i in range(4)]
    tiles += feed_forward_tiles(a["w_up_2"][0], a["w_down_2"][0])
    assert len(tiles) == TILES

    def conv_pack(w, b):
        return np.concatenate([by_partition(w), by_partition(b)[:, :, None]], 2).reshape(P, -1)

    small = {}
    for i in range(2):
        small[f"mix_norm{i}"] = by_partition(a["mix_norm"][i])
        small[f"ffn_norm{i}"] = by_partition(a["ffn_norm"][i])
        small[f"ple_norm{i}"] = by_partition(a["ple_norm"][i])
        small[f"conv{i}"] = conv_pack(a["ffn_conv_w"][i], a["ffn_conv_b"][i])
    small["conv2"] = conv_pack(a["ffn_dw_w_2"][0], a["ffn_dw_b_2"][0])
    small["hy_q"] = np.concatenate([a["hy_q_norm"][0]] * 2)[:, None]
    small["hy_k"] = np.concatenate([a["hy_k_norm"][0]] * 2)[:, None]
    sinks = a["hy_sinks"][0]
    small["sinks"] = np.broadcast_to(np.stack([sinks[:4], sinks[4:]], 1).reshape(1, 8), (P, 8))
    small["hy_conv"] = by_partition(a["hy_conv_w"][0]).reshape(P, -1)
    small["gate_bias"] = by_partition(a["gla_gate_bias"][0])
    small["o_norm"] = by_partition(a["gla_o_norm"][0])
    small["b_mod"] = by_partition(a["b_mod_2"][0])
    small["norm1"], small["norm2"] = by_partition(a["norm1_g_2"][0]), by_partition(a["norm2_g_2"][0])
    small["q_g"], small["k_g"] = a["q_norm_g_2"][0][:, None], a["k_norm_g_2"][0][:, None]
    small["dw"] = by_partition(a["conv_dw_w_2"][0]).reshape(P, -1)
    small["dw_b"] = by_partition(a["conv_dw_b_2"][0])
    small["ln_g"], small["ln_b"] = by_partition(a["conv_ln_g_2"][0]), by_partition(a["conv_ln_b_2"][0])
    small["final"] = by_partition(a["final_g_2"])
    small["c"] = np.stack([by_partition(a["c_2"][0]), by_partition(a["c_ctx_2"])], 2).reshape(P, -1)
    small["glr_w"] = a["gla_w_in"][0][:, 2048:2064].reshape(KC, P, 16).transpose(1, 0, 2).reshape(P, -1)
    params = np.ascontiguousarray(np.concatenate([small[name] for name in PARAMS], 1))

    arrays = {
        "stream": np.stack(tiles),
        "mod_stream": np.stack([columns_tile(a["w_mod_2"][0], 256 * i) for i in range(MOD_TILES)]),
        "params": params,
        "consts": constants(),
        "gate_up": np.ascontiguousarray(a["gla_w_gate_up"][0]),
        "x_in": feature_major(a["x"][0]),
        "p_in": np.ascontiguousarray(np.concatenate([feature_major(a["p"][i][0]) for i in range(2)], 1)),
        "ctx_in": feature_major(a["ctx_2"][0]),
        "pos_in": np.ascontiguousarray(np.broadcast_to(a["positions"], (P, S))),
    }
    nc = _bacc.Bacc("TRN2", target_bir_lowering=False, num_devices=1)
    args = [nc.dram_tensor(f"{name}_dram", v.shape, _mybir.dt.from_np(v.dtype), kind="ExternalInput").ap()
            for name, v in arrays.items()]
    out = nc.dram_tensor("out_dram", (P, KC, S), F32, kind="ExternalOutput").ap()
    program(nc, *args, out)
    r = _run(nc, [{f"{name}_dram": v for name, v in arrays.items()}], core_ids=[0])
    got = r.results[0]["out_dram"]
    return np.ascontiguousarray(np.moveaxis(got, (0, 1), (2, 1)).reshape(S, D))[None]
```
